# Optimizing a Trainium2 kernel written in Bass

```python
import math
import jax, jax.numpy as jnp
from jax import lax
import numpy as np

D_MODEL = 1024
BATCH = 1
SEQ = 256
DEPTH = 2

GRID_W = 64
CTX_LEN = 256
HEAD_DIM = 64
N_Q_HEADS = D_MODEL // HEAD_DIM
H_GLOBAL = N_Q_HEADS // 2
KV_GLOBAL = 2
G_GLOBAL = H_GLOBAL // KV_GLOBAL
H_LOCAL = N_Q_HEADS - H_GLOBAL
KV_LOCAL = 2
G_LOCAL = H_LOCAL // KV_LOCAL
MIX_WIDTH = (H_GLOBAL + H_LOCAL) * HEAD_DIM
WINDOW = 128
Q_BLOCK = 128
ROPE_THETA = 10000.0
N_EXPERTS = 16
N_GROUPS = 4
EXPERTS_PER_GROUP = N_EXPERTS // N_GROUPS
TOP_K = 2
D_EXPERT = D_MODEL // 2
NORM_EPS = 1e-6
ATTN_SCALE = 1.0 / math.sqrt(HEAD_DIM)
NEG_INF = -1e30
WIDTHS = (H_GLOBAL * HEAD_DIM, KV_GLOBAL * HEAD_DIM, KV_GLOBAL * HEAD_DIM,
          H_LOCAL * HEAD_DIM, KV_LOCAL * HEAD_DIM, KV_LOCAL * HEAD_DIM)
IN_WIDTH = sum(WIDTHS)
SPLIT_POINTS = tuple(int(v) for v in np.cumsum(WIDTHS)[:-1])

kernel_name = "hybrid_dit_gqa_window_sink_grouped_moe"

def _rms(x, g):
    xf = x.astype(jnp.float32)
    y = xf * lax.rsqrt(jnp.mean(xf * xf, axis=-1, keepdims=True) + NORM_EPS)
    return (y * g.astype(jnp.float32)).astype(x.dtype)

def _modulate(h, shift, scale):
    return h * (1.0 + scale) + shift

def _axial_rope_tables(n_tokens):
    rows = n_tokens // GRID_W
    row = jnp.repeat(jnp.arange(rows, dtype=jnp.int32), GRID_W).astype(jnp.float32)
    col = jnp.tile(jnp.arange(GRID_W, dtype=jnp.int32), rows).astype(jnp.float32)
    n_freq = HEAD_DIM // 4
    inv = ROPE_THETA ** (-jnp.arange(n_freq, dtype=jnp.float32) / n_freq)
    ang = jnp.stack([row[:, None] * inv, col[:, None] * inv], axis=1)
    return jnp.cos(ang), jnp.sin(ang)

def _apply_rope(x, cos, sin):
    n_freq = HEAD_DIM // 4
    shp = x.shape
    xr = x.astype(jnp.float32).reshape(shp[:-1] + (2, 2, n_freq))
    x1, x2 = xr[..., 0, :], xr[..., 1, :]
    bshape = (1, shp[1]) + (1,) * (x.ndim - 3) + (2, n_freq)
    cs, sn = cos.reshape(bshape), sin.reshape(bshape)
    out = jnp.stack([x1 * cs - x2 * sn, x2 * cs + x1 * sn], axis=-2)
    return out.reshape(shp).astype(x.dtype)

def _project(t, w_in):
    b, n = t.shape[0], t.shape[1]
    qg, kg, vg, ql, kl, vl = jnp.split(t @ w_in, SPLIT_POINTS, axis=-1)
    return (qg.reshape(b, n, KV_GLOBAL, G_GLOBAL, HEAD_DIM),
            kg.reshape(b, n, KV_GLOBAL, HEAD_DIM), vg.reshape(b, n, KV_GLOBAL, HEAD_DIM),
            ql.reshape(b, n, KV_LOCAL, G_LOCAL, HEAD_DIM),
            kl.reshape(b, n, KV_LOCAL, HEAD_DIM), vl.reshape(b, n, KV_LOCAL, HEAD_DIM))

def _attend(q, k, v, sink, mask):
    b, nq, kvh, g, d = q.shape
    n = k.shape[1]
    s = jnp.einsum('bqkgd,bnkd->bkgqn', q, k, preferred_element_type=jnp.float32) * ATTN_SCALE
    if mask is not None:
        s = jnp.where(mask, s, NEG_INF)
    if sink is not None:
        sk = jnp.broadcast_to(sink.astype(jnp.float32).reshape(1, kvh, g, 1, 1), s.shape[:-1] + (1,))
        s = jnp.concatenate([s, sk], axis=-1)
    p = jax.nn.softmax(s, axis=-1)[..., :n].astype(v.dtype)
    o = jnp.einsum('bkgqn,bnkd->bqkgd', p, v)
    return o.reshape(b, nq, kvh * g * d)

def _global_latent(q, k, v, kc, vc):
    b, s, kvh, g, d = q.shape
    nblk = s // Q_BLOCK
    k_all = jnp.concatenate([kc, k], axis=1)
    v_all = jnp.concatenate([vc, v], axis=1)
    qb = q.reshape(b, nblk, Q_BLOCK, kvh, g, d).transpose(1, 0, 2, 3, 4, 5)
    o = lax.map(lambda qi: _attend(qi, k_all, v_all, None, None), qb)
    return o.transpose(1, 0, 2, 3).reshape(b, s, kvh * g * d)

def _local_latent(q, k, v, kc, vc, sink):
    b, s, kvh, g, d = q.shape
    nblk = s // Q_BLOCK
    span = Q_BLOCK + 2 * WINDOW
    pad = ((0, 0), (WINDOW, WINDOW), (0, 0), (0, 0))
    kp, vp = jnp.pad(k, pad), jnp.pad(v, pad)
    qb = q.reshape(b, nblk, Q_BLOCK, kvh, g, d).transpose(1, 0, 2, 3, 4, 5)
    qi_idx = jnp.arange(Q_BLOCK, dtype=jnp.int32)[:, None]
    kj_idx = jnp.arange(span, dtype=jnp.int32)[None, :]
    band = jnp.abs(kj_idx - WINDOW - qi_idx) <= WINDOW
    ctx_ok = jnp.ones((Q_BLOCK, kc.shape[1]), dtype=bool)

    def block(args):
        qi, n = args
        start = n * Q_BLOCK
        kb = lax.dynamic_slice_in_dim(kp, start, span, axis=1)
        vb = lax.dynamic_slice_in_dim(vp, start, span, axis=1)
        key_pos = start - WINDOW + kj_idx
        valid = band & (key_pos >= 0) & (key_pos < s)
        mask = jnp.concatenate([valid, ctx_ok], axis=-1)
        return _attend(qi, jnp.concatenate([kb, kc], axis=1), jnp.concatenate([vb, vc], axis=1), sink, mask)

    o = lax.map(block, (qb, jnp.arange(nblk, dtype=jnp.int32)))
    return o.transpose(1, 0, 2, 3).reshape(b, s, kvh * g * d)

def _token_mixers(h, hc, w_in, qn_g, kn_g, qn_l, kn_l, sink, cos, sin, with_ctx_out):
    qg, kg, vg, ql, kl, vl = _project(h, w_in)
    qgc, kgc, vgc, qlc, klc, vlc = _project(hc, w_in)
    qg = _apply_rope(_rms(qg, qn_g), cos, sin)
    kg = _apply_rope(_rms(kg, kn_g), cos, sin)
    ql = _apply_rope(_rms(ql, qn_l), cos, sin)
    kl = _apply_rope(_rms(kl, kn_l), cos, sin)
    qgc, kgc = _rms(qgc, qn_g), _rms(kgc, kn_g)
    qlc, klc = _rms(qlc, qn_l), _rms(klc, kn_l)
    y = jnp.concatenate([_global_latent(qg, kg, vg, kgc, vgc),
                         _local_latent(ql, kl, vl, klc, vlc, sink)], axis=-1)
    if not with_ctx_out:
        return y, None
    yc = jnp.concatenate([_attend(qgc, kgc, vgc, None, None),
                          _attend(qlc, klc, vlc, sink, None)], axis=-1)
    return y, yc

def _grouped_moe(t, router_w, router_b, w_gate, w_up, w_down):
    n = t.shape[0]
    scores = jax.nn.sigmoid((t @ router_w).astype(jnp.float32))
    sel = scores + router_b.astype(jnp.float32)
    grp_score = lax.top_k(sel.reshape(n, N_GROUPS, EXPERTS_PER_GROUP), TOP_K)[0].sum(-1)
    g_idx = lax.top_k(grp_score, 1)[1][:, 0]
    in_group = jnp.repeat(jax.nn.one_hot(g_idx, N_GROUPS, dtype=jnp.float32), EXPERTS_PER_GROUP, axis=-1) > 0
    e_idx = lax.top_k(jnp.where(in_group, sel, -jnp.inf), TOP_K)[1]
    w = jnp.take_along_axis(scores, e_idx, axis=-1)
    w = w / jnp.sum(w, axis=-1, keepdims=True)
    gates = jnp.sum(jax.nn.one_hot(e_idx, N_EXPERTS, dtype=jnp.float32) * w[..., None], axis=1)
    y = jnp.zeros(t.shape, jnp.float32)
    for e in range(N_EXPERTS):
        he = jax.nn.silu(t @ w_gate[e]) * (t @ w_up[e])
        y = y + gates[:, e:e + 1] * (he @ w_down[e]).astype(jnp.float32)
    return y.astype(t.dtype)

def setup_inputs(seed: int = 0) -> dict:
    key = jax.random.key(seed)
    ks = jax.random.split(key, 20)
    L, D, E, F = DEPTH, D_MODEL, N_EXPERTS, D_EXPERT

    def nrm(k, shape, s):
        return jax.random.normal(k, shape, jnp.float32) * s

    return {
        "x": nrm(ks[0], (BATCH, SEQ, D), 1.0),
        "c": nrm(ks[1], (BATCH, D), 1.0),
        "ctx": nrm(ks[2], (BATCH, CTX_LEN, D), 1.0),
        "c_ctx": nrm(ks[3], (D,), 1.0),
        "ada_w": nrm(ks[4], (L, D, 6 * D), 0.5 * D ** -0.5),
        "ada_b": nrm(ks[5], (L, 6 * D), 0.02),
        "attn_norm_g": 1.0 + nrm(ks[6], (L, D), 0.02),
        "ffn_norm_g": 1.0 + nrm(ks[7], (L, D), 0.02),
        "w_in": nrm(ks[8], (L, D, IN_WIDTH), D ** -0.5),
        "qn_global": 1.0 + nrm(ks[9], (L, HEAD_DIM), 0.02),
        "kn_global": 1.0 + nrm(ks[10], (L, HEAD_DIM), 0.02),
        "qn_local": 1.0 + nrm(ks[11], (L, HEAD_DIM), 0.02),
        "kn_local": 1.0 + nrm(ks[12], (L, HEAD_DIM), 0.02),
        "sink_logit": nrm(ks[13], (L, H_LOCAL), 0.5),
        "w_out": nrm(ks[14], (L, MIX_WIDTH, D), MIX_WIDTH ** -0.5),
        "router_w": nrm(ks[15], (D, E), D ** -0.5),
        "router_b": nrm(ks[16], (E,), 0.01),
        "w_gate": nrm(ks[17], (L, E, D, F), D ** -0.5),
        "w_up": nrm(ks[18], (L, E, D, F), D ** -0.5),
        "w_down": nrm(ks[19], (L, E, F, D), F ** -0.5),
    }

def reference(x, c, ctx, c_ctx, ada_w, ada_b, attn_norm_g, ffn_norm_g, w_in, qn_global, kn_global,
              qn_local, kn_local, sink_logit, w_out, router_w, router_b, w_gate, w_up, w_down):
    b, s, d = x.shape
    n_ctx = ctx.shape[1]
    cos, sin = _axial_rope_tables(s)
    silu_c = jax.nn.silu(c)
    silu_cc = jax.nn.silu(c_ctx)
    xc = ctx
    for l in range(DEPTH):
        need_ctx = l < DEPTH - 1
        sh1, sc1, g1, sh2, sc2, g2 = [m[:, None, :] for m in jnp.split(silu_c @ ada_w[l] + ada_b[l], 6, axis=-1)]
        sh1c, sc1c, g1c, sh2c, sc2c, g2c = jnp.split(silu_cc @ ada_w[l] + ada_b[l], 6, axis=-1)
        h = _modulate(_rms(x, attn_norm_g[l]), sh1, sc1)
        hc = _modulate(_rms(xc, attn_norm_g[l]), sh1c, sc1c)
        y, yc = _token_mixers(h, hc, w_in[l], qn_global[l], kn_global[l], qn_local[l], kn_local[l],
                              sink_logit[l], cos, sin, need_ctx)
        x = x + g1 * (y @ w_out[l])
        h = _modulate(_rms(x, ffn_norm_g[l]), sh2, sc2)
        if need_ctx:
            xc = xc + g1c * (yc @ w_out[l])
            hc = _modulate(_rms(xc, ffn_norm_g[l]), sh2c, sc2c)
            tokens = jnp.concatenate([h.reshape(b * s, d), hc.reshape(b * n_ctx, d)], axis=0)
            yf = _grouped_moe(tokens, router_w, router_b, w_gate[l], w_up[l], w_down[l])
            x = x + g2 * yf[:b * s].reshape(b, s, d)
            xc = xc + g2c * yf[b * s:].reshape(b, n_ctx, d)
        else:
            yf = _grouped_moe(h.reshape(b * s, d), router_w, router_b, w_gate[l], w_up[l], w_down[l])
            x = x + g2 * yf.reshape(b, s, d)
    return x


_drawn_inputs = setup_inputs


def setup_inputs(seed=0):
    import zlib

    import numpy as np

    out = dict(_drawn_inputs(seed))
    spreads = {}
    factors = {'attn_norm_g': 6.487,
     'qn_global': 8.0,
     'kn_global': 8.0,
     'qn_local': 8.0,
     'kn_local': 8.0,
     'sink_logit': 8.0}
    for name, (base, spread) in spreads.items():
        noise = np.random.default_rng([zlib.crc32(name.encode()), seed]).standard_normal(out[name].shape)
        drawn = base * np.exp(spread * noise) if base else spread * noise
        out[name] = __import__('jax').numpy.asarray(drawn.astype(out[name].dtype))
    for name, factor in factors.items():
        out[name] = (out[name] * factor).astype(out[name].dtype)
    return out
```

```python
from contextlib import ExitStack

import concourse.bass as bass
from concourse import mybir

F32 = mybir.dt.float32
I32 = mybir.dt.int32
U32 = mybir.dt.uint32
ALU = mybir.AluOpType
ACT = mybir.ActivationFunctionType
AX = mybir.AxisListType

P = 128
D = 1024
KD = D // P
SEQ = 256
CTX = 256
DEPTH = 2
HD = 64
IN_W = 1536
NE = 16
NG = 4
EPG = NE // NG
FE = 512
KF = FE // P
NMOD = 6 * KD
EPS = 1e-6
SCALE = HD ** -0.5
NEG = -1e30
CHUNK = 64
MAXCH = 512 // CHUNK
BIG = 1e30

TOK_TILES = [(SEQ + CTX) // P, SEQ // P]
UNITS = [16 * t for t in TOK_TILES]
MAX_CHUNKS = [NE + 2 * t * P // CHUNK for t in TOK_TILES]

C_ID, C_UP, C_BLK, C_SWP = 0, P, 2 * P, 3 * P
C_COS = 4 * P
C_SIN = C_COS + SEQ
C_M0 = C_SIN + SEQ
C_M1 = C_M0 + P
C_IOTA = C_M1 + P
C_TRI = C_IOTA + CHUNK
C_THR = C_TRI + (NE + 1) * NE
C_W16 = C_THR + MAXCH - 1
C_W4 = C_W16 + NE
C_END = C_W4 + NG

V_ADAB = 0
V_AG = DEPTH * NMOD
V_FG = V_AG + DEPTH * KD
V_C = V_FG + DEPTH * KD
V_CC = V_C + KD
V_QN = V_CC + KD
V_END = V_QN + 4 * DEPTH


def constants():
    import numpy as np
    t = np.zeros((P, C_END), np.float32)
    i = np.arange(P)
    t[:, C_ID:C_ID + P] = np.eye(P)
    t[:, C_UP:C_UP + P] = i[:, None] < i[None, :]
    t[:, C_BLK:C_BLK + P] = i[:, None] // HD == i[None, :] // HD
    t[:, C_SWP:C_SWP + P] = (i[:, None] ^ 16) == i[None, :]
    tok = np.arange(SEQ)
    grid = np.stack([tok // 64, tok % 64]).astype(np.float32)
    nf = HD // 4
    inv = np.float32(10000.0) ** (-np.arange(nf, dtype=np.float32) / np.float32(nf))
    d = i % HD
    ang = (grid[d // 32] * inv[d % nf][:, None]).astype(np.float32)
    t[:, C_COS:C_COS + SEQ] = np.cos(ang)
    t[:, C_SIN:C_SIN + SEQ] = np.where((d % 32 < 16)[:, None], -np.sin(ang), np.sin(ang))
    t[:, C_M0:C_M0 + P] = np.where(i[None, :] > i[:, None], NEG, 0.0)
    t[:, C_M1:C_M1 + P] = np.where(i[None, :] < i[:, None], NEG, 0.0)
    t[:, C_IOTA:C_IOTA + CHUNK] = np.arange(CHUNK)
    e = np.arange(NE)
    t[:, C_TRI:C_THR] = (e[None, :] < np.arange(NE + 1)[:, None]).reshape(-1)
    t[:, C_THR:C_W16] = CHUNK * np.arange(1, MAXCH)
    t[:, C_W16:C_W4] = NE - e
    t[:, C_W4:C_END] = NG - np.arange(NG)
    return t


def backbone(nc, x, c, ctx_in, c_ctx, ada_w, ada_b, attn_norm_g, ffn_norm_g, w_in, qn_global, kn_global,
             qn_local, kn_local, sink_logit, w_out, router_w, router_b, w_gate, w_up, w_down, table, out):
    with ExitStack() as stack:
        def sb(name, shape, dt=F32):
            return stack.enter_context(nc.sbuf_tensor(name, shape, dt))

        def sem(name):
            return stack.enter_context(nc.semaphore(name))

        def per_layer(name):
            return [sem(f"{name}{l}") for l in range(DEPTH)]

        ring = sb("ring", [P, 9, 4096])
        x_t = sb("x_t", [P, KD, 512])
        h_t = sb("h_t", [P, KD, 512])
        tokm = sb("tokm", [P, 4, D])
        cst = sb("cst", [P, C_END])
        ones = sb("ones", [P, P])
        eps = sb("eps", [P, 2])
        rw = sb("rw", [P, KD, NE])
        rb = sb("rb", [P, NE])
        sink = sb("sink", [P, DEPTH * 8])
        nsink = sb("nsink", [P, DEPTH * 8])
        work = sb("work", [P, 1536])
        vec = sb("vec", [P, V_END])
        scv = sb("scv", [P, KD, 2])
        mods = sb("mods", [P, DEPTH * NMOD, 2])
        gain = sb("gain", [P, DEPTH, 2, KD, 2])
        posrel = sb("posrel", [P, 8])
        posidx = sb("posidx", [P, 8], U32)
        wgt = sb("wgt", [P, 8])
        first = sb("first", [P, NE + 1], I32)

        bank = [stack.enter_context(nc.psum_tensor(f"bank{i}", [P, 512], F32)) for i in range(8)]
        y_rows = nc.dram_tensor("y_rows", [(max(MAX_CHUNKS) + 1) * CHUNK, D], F32, kind="Internal").ap()

        ident = cst[:, C_ID:C_ID + P]
        upper = cst[:, C_UP:C_UP + P]
        head_ones = cst[:, C_BLK:C_BLK + P]
        swap = cst[:, C_SWP:C_SWP + P]
        cos = cst[:, C_COS:C_COS + SEQ]
        sin = cst[:, C_SIN:C_SIN + SEQ]
        band = [cst[:, C_M0:C_M0 + P], cst[:, C_M1:C_M1 + P]]
        iota = cst[:, C_IOTA:C_IOTA + CHUNK]

        vec_a = h_t[0:96, 0, 0:P]
        vec_b = h_t[0:V_END - 96, 0, P:2 * P]
        sq = [work[:, 0:512], work[:, 512:1024]]
        rstd = work[:, 1024:1536]
        win = ring[:, 3:6, :].rearrange("p a b -> p (a b)").rearrange("p (k n) -> p k n", k=KD)
        wout = [ring[:, 6, :].rearrange("p (k n) -> p k n", k=4), ring[:, 3, :].rearrange("p (k n) -> p k n", k=4)]
        scratch = ring[:, 7:9, :].rearrange("p a b -> p (a b)")
        qk_t = scratch[:, 0:5120].rearrange("p (i n) -> p i n", i=10)
        v_tok = scratch[:, 5120:6144].rearrange("p (t n) -> p t n", t=4)
        probs = scratch[:, 6144:8192].rearrange("p (b n) -> p b n", b=4)
        rope_a = probs[:, 0, 0:SEQ]
        rope_b = probs[:, 1, 0:SEQ]
        probs_t = h_t[:, 0:2, :]
        smx = h_t[:, 2, 0:64]
        negmax = h_t[:, 2, 64:128]
        lsum = h_t[:, 2, 128:192]
        esink = h_t[:, 2, 192:256]
        zeros = h_t[:, 3:5, :].rearrange("p k n -> p (k n)")
        ltot = h_t[:, 2, 256:260]
        lrec = h_t[:, 2, 264:268]
        hflat = h_t[:, :, :].rearrange("p k n -> p (k n)")
        pick = hflat[:, 0:256]
        pick2 = hflat[:, 256:768]
        hc_t = hflat[:, 768:1280]
        act_g = hflat[:, 1280:1536]
        he_t = hflat[:, 1536:1792]
        yc_t = hflat[:, 1792:2304]
        yrow = hflat[:, 2304:2816]
        ych = [tokm, hflat.rearrange("p (t n) -> p t n", t=4)]
        out_tok = ring[:, 0:1, :].rearrange("p a b -> p (a b)")[:, 0:2 * D].rearrange("p (t n) -> p t n", t=2)

        cst_in, vec_in, x_in, small_in = sem("cst_in"), sem("vec_in"), sem("x_in"), sem("small_in")
        ada_in = [sem(f"ada_in{s}") for s in range(4)]
        ada2_in = [sem(f"ada2_in{s}") for s in range(4)]
        win_in = [sem(f"win_in{s}") for s in range(4)]
        wout_in = [sem(f"wout_in{s}") for s in range(2)]
        ew_in = [[sem(f"ew_in{l}_{s}") for s in range(9)] for l in range(DEPTH)]
        set_free = [[sem(f"set_free{l}_{s}") for s in range(3)] for l in range(DEPTH)]
        ones_set = sem("ones_set")
        vec_turned, vec_ready, silu_ready = sem("vec_turned"), sem("vec_ready"), sem("silu_ready")
        x_turned, xt_act, xt_dve = sem("x_turned"), sem("xt_act"), sem("xt_dve")
        ada_used, mods_ready = sem("ada_used"), sem("mods_ready")
        sq_ready, sq_used, hs_ready, h_ready = sem("sq_ready"), sem("sq_used"), sem("hs_ready"), sem("h_ready")
        norm_root, qk_root = sem("norm_root"), sem("qk_root")
        qk_mm, qk_evac, qk_stats, qk_done = sem("qk_mm"), sem("qk_evac"), sem("qk_stats"), sem("qk_done")
        v_mm, v_ready, swapped = sem("v_mm"), sem("v_ready"), sem("swapped")
        sc_done, max_ready, exp_done = sem("sc_done"), sem("max_ready"), sem("exp_done")
        p_turned, pt_ready, pv_done, y_evac = sem("p_turned"), sem("pt_ready"), sem("pv_done"), sem("y_evac")
        y_turned, yt_act, yt_dve = sem("y_turned"), sem("yt_act"), sem("yt_dve")
        wo_mm, xw_ready = sem("wo_mm"), sem("xw_ready")
        lg_mm, sig_ready, h_turned, tok_ready = sem("lg_mm"), sem("sig_ready"), sem("h_turned"), sem("tok_ready")
        mask_ready, rank_mm, route_ready = sem("mask_ready"), sem("rank_mm"), sem("route_ready")
        pick_ready, gather_mm, hc_ready = per_layer("pick_ready"), per_layer("gather_mm"), per_layer("hc_ready")
        gate_mm, up_mm, silu_done = per_layer("gate_mm"), per_layer("up_mm"), per_layer("silu_done")
        he_ready, down_mm, yc_ready = per_layer("he_ready"), per_layer("down_mm"), per_layer("yc_ready")
        rows_turned, rows_ready, rows_stored = per_layer("rows_turned"), per_layer("rows_ready"), per_layer("rows_stored")
        zeros_set, zero_stored = sem("zeros_set"), sem("zero_stored")
        rows_all, bufs_free = sem("rows_all"), sem("bufs_free")
        loop_step = per_layer("loop_step")
        yg_in = [[sem(f"yg_in{l}_{t}") for t in range(4)] for l in range(DEPTH)]
        y_scaled, y_summed, c_turned, xc_ready = sem("y_scaled"), sem("y_summed"), sem("c_turned"), sem("xc_ready")
        o_turned, o_act, o_dve, out_done = sem("o_turned"), sem("o_act"), sem("o_dve"), sem("out_done")
        dve_step = sem("dve_step")

        def units(l):
            return [(tt, T, kv, r) for tt in range(TOK_TILES[l]) for T in range(2) for kv in range(2)
                    for r in range(4)]

        def keys(tt):
            return (0, 512) if tt < 2 else (256, 256)

        def expert_weights(e, a):
            return [(3 * a, w_gate, KD), (3 * a + 1, w_up, KD), (3 * a + 2, w_down, KF)]

        block = stack.enter_context(nc.Block())

        @block.sync
        def _(sp):
            def slot(s, k):
                return ring[:, s, :].rearrange("p (k n) -> p k n", k=k)

            def load_ada(s, u, signal):
                l, m = divmod(u, 12)
                sp.dma_start(slot(s, KD), ada_w[l, :, m * 512:m * 512 + 512].rearrange("(k p) n -> p k n", p=P)
                             ).then_inc(signal, 16)

            def load_win(l):
                for q in range(4):
                    sp.dma_start(win[:, 2 * q:2 * q + 2, :],
                                 w_in[l, 256 * q:256 * q + 256, :].rearrange("(k p) n -> p k n", p=P)
                                 ).then_inc(win_in[q], 16)

            def load_wout(l, half):
                sp.dma_start(wout[half], w_out[l, 512 * half:512 * half + 512, :].rearrange("(k p) n -> p k n", p=P)
                             ).then_inc(wout_in[half], 16)

            def load_expert(l, e, a, parts=(0, 1, 2)):
                for part in parts:
                    s, w, k = expert_weights(e, a)[part]
                    src = w[l, bass.ds(e, 1)].rearrange("a (k p) n -> p (a k) n", p=P)
                    sp.dma_start(slot(s, k), src).then_inc(ew_in[l][s], 16)

            for u, s in enumerate((6, 0, 1, 2)):
                load_ada(s, u, ada_in[u])
            load_win(0)
            for part in range(3):
                sp.wait_ge(ada_used, part + 2)
                load_expert(0, 0, 0, (part,))
            for u in range(4, 24):
                if u == 5:
                    sp.wait_ge(v_mm, 2)
                if u >= 8:
                    sp.wait_ge(ada_used, u - 3)
                load_ada((6, 3, 4, 5)[u % 4], u, ada2_in[u % 4])
            for l in range(DEPTH):
                if l == 0:
                    sp.wait_ge(ada_used, 21)
                    load_wout(0, 0)
                    sp.wait_ge(ada_used, 22)
                    load_wout(0, 1)
                    sp.wait_ge(ada_used, 24)
                else:
                    sp.wait_ge(set_free[0][1], 5)
                    load_win(1)
                    sp.wait_ge(set_free[0][2], 5)
                    load_wout(1, 0)
                    sp.wait_ge(set_free[0][0], 6)
                    load_expert(1, 0, 0)
                    sp.wait_ge(v_mm, 4)
                    load_wout(1, 1)
                load_expert(l, 1, 1, (1, 2))
                sp.wait_ge(pv_done, sum(UNITS[:l + 1]))
                load_expert(l, 2, 2, (1, 2))
                sp.wait_ge(wo_mm, KD * (l + 1))
                load_expert(l, 1, 1, (0,))
                load_expert(l, 2, 2, (0,))
                with sp.Fori(1, 5) as i:
                    for a in range(3):
                        sp.wait_ge(set_free[l][a], i)
                        load_expert(l, 3 * i + a, a)
                sp.wait_ge(set_free[l][0], 5)
                load_expert(l, 15, 0)
            for tt in range(2):
                sp.wait_ge(o_act, tt + 1)
                sp.wait_ge(o_dve, tt + 1)
                sp.dma_start(out[0, P * tt:P * tt + P, :], out_tok[:, tt, :]).then_inc(out_done, 16)
            sp.wait_ge(out_done, 32)

        @block.tensor
        def _(pe):
            mm = nc.tensor.matmul
            turn = nc.tensor.transpose

            def ada_unit(u):
                if u < 4:
                    s = (6, 0, 1, 2)[u]
                    pe.wait_ge(ada_in[u], 16)
                else:
                    s = (6, 3, 4, 5)[u % 4]
                    pe.wait_ge(ada2_in[u % 4], 16 * (u // 4))
                if u == 4:
                    pe.wait_ge(mods_ready, 1)
                w = ring[:, s, :].rearrange("p (k n) -> p k n", k=KD)
                for m in range(4):
                    col = 2 * (4 * u + m)
                    for k in range(KD):
                        last = mm(bank[7][:, col:col + 2], w[:, k, P * m:P * m + P], scv[:, k, :],
                                  start=(k == 0), stop=(k == KD - 1))
                last.then_inc(ada_used, 1)

            def norm_sums(n, width):
                for k in range(KD):
                    pe.wait_ge(sq_ready, KD * n + k + 1)
                    mm(bank[0][:, 0:width], ones[:, :], sq[k % 2][:, 0:width],
                       start=(k == 0), stop=(k == KD - 1)).then_inc(sq_used, 1)

            def qk_weights(i, k):
                T, j = divmod(i - 2, 4)
                col = 512 + 768 * i if i < 2 else 768 * T + P * j
                return win[:, k, col:col + P]

            def qk_sums(l, i, n):
                pe.wait_ge(qk_evac, 10 * l + i + 1)
                if 10 * l + i > 0:
                    pe.wait_ge(qk_done, 10 * l + i)
                mm(bank[3][:, 0:n], head_ones, sq[i % 2][:, 0:n], start=True, stop=True)
                mm(bank[4][:, 0:SEQ], swap, qk_t[:, i, 0:SEQ], start=True, stop=True).then_inc(qk_stats, 1)

            def qkv(l):
                widths = [512, 512] + [P * TOK_TILES[l]] * 8
                for i in range(10):
                    if i >= 2:
                        pe.wait_ge(qk_evac, 10 * l + i - 1)
                    for k in range(KD):
                        if i == 0:
                            pe.wait_ge(h_ready, 2 * KD * l + k + 1)
                            pe.wait_ge(win_in[k // 2], 16 * (l + 1))
                        last = mm(bank[1 + i % 2][:, 0:widths[i]], qk_weights(i, k), h_t[:, k, 0:widths[i]],
                                  start=(k == 0), stop=(k == KD - 1))
                    last.then_inc(qk_mm, 1)
                    if i >= 1:
                        qk_sums(l, i - 1, widths[i - 1])
                for tt in range(4):
                    for k in range(KD):
                        wv = win[:, k, :].rearrange("p (h n) -> p h n", h=2)[:, :, 640:768]
                        o = bank[5 + tt // 2][:, 256 * (tt % 2):256 * (tt % 2) + 256].rearrange("p (h n) -> p h n", h=2)
                        last = mm(o, h_t[:, k, P * tt:P * tt + P], wv, start=(k == 0), stop=(k == KD - 1))
                    if tt % 2:
                        last.then_inc(v_mm, 1)
                    if tt == 0:
                        qk_sums(l, 9, widths[9])

            def attention(l):
                ub, gb = sum(UNITS[:l]), sum(UNITS[:l]) // 4
                us = units(l)

                def scores(n):
                    tt, T, kv, r = us[n]
                    k0, kn = keys(tt)
                    if n == 0:
                        pe.wait_ge(qk_done, 10 * (l + 1))
                        pe.wait_ge(swapped, 64 * (l + 1))
                    if n >= 3:
                        pe.wait_ge(exp_done, ub + n - 2)
                    a = r % 2
                    rows = slice(HD * a, HD * a + HD)
                    k_t = (qk_t[:, T] if a == kv else sq[T])[rows, k0:k0 + kn]
                    q_t = qk_t[rows, 2 + 4 * T + 2 * kv + r // 2, P * tt:P * tt + P]
                    o = bank[n % 3]
                    parts = [(0, kn, False)]
                    if T == 1 and tt < 2:
                        parts = ([(0, P, False), (P, 2 * P, True), (2 * P, kn, False)] if tt == 0 else
                                 [(0, P, True), (P, kn, False)])
                    for c0, c1, masked in parts:
                        last = mm(o[:, c0:c1], q_t, k_t[:, c0:c1], start=True, stop=not masked)
                        if masked:
                            last = mm(o[:, c0:c1], ident, band[tt], start=False, stop=True)
                    last.then_inc(sc_done, 1)

                def turn_probs(n):
                    tt = us[n][0]
                    pe.wait_ge(exp_done, ub + n + 1)
                    if n >= 2:
                        pe.wait_ge(pt_ready, ub + n - 1)
                    for q in range(keys(tt)[1] // P):
                        last = turn(bank[4 + n % 2][:, P * q:P * q + P], probs[:, n % 4, P * q:P * q + P], ident)
                    last.then_inc(p_turned, 1)

                def values(n):
                    tt, T, kv, r = us[n]
                    k0, kn = keys(tt)
                    g = n // 4
                    pe.wait_ge(pt_ready, ub + n + 1)
                    if n == 0:
                        pe.wait_ge(v_ready, 2 * (l + 1))
                    if r == 0 and g >= 2:
                        pe.wait_ge(y_evac, gb + g - 1)
                    nk = kn // P
                    for q in range(nk):
                        col = P * T + HD * kv
                        last = mm(bank[(3, 6)[g % 2]][:, HD * r:HD * r + HD], probs_t[:, n % 2, P * q:P * q + P],
                                  v_tok[:, k0 // P + q, col:col + HD], start=(q == 0), stop=(q == nk - 1))
                    last.then_inc(pv_done, 1)

                for n in range(UNITS[l] + 3):
                    if n < UNITS[l]:
                        scores(n)
                    if 2 <= n < UNITS[l] + 2:
                        turn_probs(n - 2)
                    if n >= 3:
                        values(n - 3)
                    if l == 0 and n % 3 == 1 and n // 3 < 20:
                        ada_unit(4 + n // 3)

            def project_out(l):
                nt = TOK_TILES[l]
                pe.wait_ge(y_evac, sum(UNITS[:l + 1]) // 4)
                for m in range(KD):
                    if m >= 2:
                        pe.wait_ge((yt_act, yt_dve)[m % 2], 4 * l + m // 2)
                    for tt in range(nt):
                        last = turn(bank[1 + m % 2][:, P * tt:P * tt + P], tokm[:, tt, P * m:P * m + P], ident)
                    last.then_inc(y_turned, 1)
                for m in range(KD):
                    if m >= 2:
                        pe.wait_ge(xw_ready, KD * l + m - 1)
                    for k in range(KD):
                        if m == 0:
                            pe.wait_ge((yt_act, yt_dve)[k % 2], 4 * l + k // 2 + 1)
                            pe.wait_ge(wout_in[k // 4], 16 * (l + 1))
                        last = mm(bank[4 + m % 2][:, 0:P * nt], wout[k // 4][:, k % 4, P * m:P * m + P],
                                  h_t[:, k, 0:P * nt], start=(k == 0), stop=(k == KD - 1))
                    last.then_inc(wo_mm, 1)

            def route(l):
                nt = TOK_TILES[l]
                tb = 2 * sum(TOK_TILES[:l])
                for tt in range(nt):
                    for k in range(KD):
                        if tt == 0:
                            pe.wait_ge(h_ready, KD * (2 * l + 1) + k + 1)
                        last = mm(bank[1][:, NE * tt:NE * tt + NE], h_t[:, k, P * tt:P * tt + P], rw[:, k, :],
                                  start=(k == 0), stop=(k == KD - 1))
                last.then_inc(lg_mm, 1)
                for q in range(2 * nt):
                    if q >= 4:
                        pe.wait_ge(tok_ready, tb + q - 3)
                    for k in range(4):
                        kk = 4 * (q % 2) + k
                        last = turn(bank[2 + q % 4][:, P * k:P * k + P], h_t[:, kk, P * (q // 2):P * (q // 2) + P], ident)
                    last.then_inc(h_turned, 1)
                pe.wait_ge(mask_ready, l + 1)
                mask = work[:, 0:NE * nt].rearrange("p (t e) -> p t e", t=nt)
                for tt in range(nt):
                    for t2 in range(tt + 1):
                        mm(bank[6][:, NE * tt:NE * tt + NE], upper if t2 == tt else ones[:, :], mask[:, t2, :],
                           start=(t2 == 0), stop=(t2 == tt))
                for t2 in range(nt):
                    last = mm(bank[6][:, NE * nt:NE * nt + NE], ones[:, :], mask[:, t2, :],
                              start=(t2 == 0), stop=(t2 == nt - 1))
                last.then_inc(rank_mm, 1)

            def experts(l):
                nt = TOK_TILES[l]

                def gather(n):
                    pe.wait_ge(pick_ready[l], n + 1)
                    for k in range(KD):
                        for tt in range(nt):
                            last = mm(bank[0][:, CHUNK * k:CHUNK * k + CHUNK], tokm[:, tt, P * k:P * k + P],
                                      pick[:, CHUNK * tt:CHUNK * tt + CHUNK], start=(tt == 0), stop=(tt == nt - 1))
                    last.then_inc(gather_mm[l], 1)

                def turn_rows(n):
                    pe.wait_ge(yc_ready[l], n + 1)
                    pe.wait_ge(rows_ready[l], n + 1)
                    for j in range(KD // 2):
                        last = turn(bank[4][:, P * j:P * j + P], yc_t[:, P * j:P * j + P], ident)
                    last.then_inc(rows_turned[l], 1)

                def chunk(a, turns, g):
                    wg, wu = (ring[:, 3 * a + s, :].rearrange("p (k n) -> p k n", k=KD) for s in range(2))
                    wd = ring[:, 3 * a + 2, :].rearrange("p (k n) -> p k n", k=KF)
                    pe.wait_ge(hc_ready[l], g + 1)
                    for s, w, signal in ((0, wg, gate_mm[l]), (1, wu, up_mm[l])):
                        pe.wait_ge(ew_in[l][3 * a + s], 16 * turns)
                        for m in range(KF):
                            for k in range(KD):
                                last = mm(bank[1 + s][:, CHUNK * m:CHUNK * m + CHUNK], w[:, k, P * m:P * m + P],
                                          hc_t[:, CHUNK * k:CHUNK * k + CHUNK], start=(k == 0), stop=(k == KD - 1))
                        last.then_inc(signal, 1)
                    turn_rows(g)
                    gather(g + 1)
                    pe.wait_ge(ew_in[l][3 * a + 2], 16 * turns)
                    pe.wait_ge(he_ready[l], g + 1)
                    for m in range(KD):
                        for k in range(KF):
                            last = mm(bank[3][:, CHUNK * m:CHUNK * m + CHUNK], wd[:, k, P * m:P * m + P],
                                      he_t[:, CHUNK * k:CHUNK * k + CHUNK], start=(k == 0), stop=(k == KF - 1))
                    last.then_inc(down_mm[l], 1)

                def expert(e, a, turns):
                    g0 = pe.value_load(first[0:1, bass.ds(e, 1)], min_val=0, max_val=MAX_CHUNKS[l])
                    g1 = pe.value_load(first[0:1, bass.ds(e + 1, 1)], min_val=0, max_val=MAX_CHUNKS[l])
                    with pe.Fori(g0, g1) as g:
                        chunk(a, turns, g)
                    mm(bank[6][:, 0:1], ones[:, :], ones[:, 0:1], start=True, stop=True).then_inc(set_free[l][a], 1)

                pe.wait_ge(route_ready, l + 1)
                pe.wait_ge(tok_ready, 2 * sum(TOK_TILES[:l + 1]))
                gather(0)
                with pe.Fori(0, 5) as i:
                    for a in range(3):
                        expert(3 * i + a, a, i + 1)
                expert(15, 0, 6)
                total = pe.value_load(first[0:1, NE:NE + 1], min_val=1, max_val=MAX_CHUNKS[l])
                turn_rows(total)

            def combine(l):
                nt = TOK_TILES[l]
                tb = sum(TOK_TILES[:l])
                for tt in range(nt):
                    pe.wait_ge(y_summed, tb + tt + 1)
                    if tt >= 2:
                        pe.wait_ge(xc_ready, tb + tt - 1)
                    for k in range(KD):
                        col = 512 * (k % 2) + P * (k // 2)
                        last = turn(bank[1 + 2 * (tt % 2) + k // 4][:, P * (k % 4):P * (k % 4) + P],
                                    tokm[:, tt, col:col + P], ident)
                    last.then_inc(c_turned, 1)

            pe.wait_ge(cst_in, 16)
            pe.wait_ge(vec_in, 16 * 14)
            turn(bank[0][:, 0:96], vec_a, ident[0:96, 0:96])
            turn(bank[0][:, 96:V_END], vec_b, ident[0:V_END - 96, 0:V_END - 96]).then_inc(vec_turned, 1)
            pe.wait_ge(x_in, 32)
            for k in range(KD):
                if k >= 6:
                    pe.wait_ge((xt_act, xt_dve)[k % 2], 1)
                for tt in range(4):
                    last = turn(bank[1 + k % 6][:, P * tt:P * tt + P], tokm[:, tt, P * k:P * k + P], ident)
                last.then_inc(x_turned, 1)
            pe.wait_ge(ones_set, 1)
            pe.wait_ge(silu_ready, 1)
            for l in range(DEPTH):
                norm_sums(2 * l, 512)
                if l == 0:
                    for u in range(4):
                        ada_unit(u)
                qkv(l)
                attention(l)
                project_out(l)
                norm_sums(2 * l + 1, P * TOK_TILES[l])
                if l == 0:
                    pe.wait_ge(small_in, 32)
                route(l)
                experts(l)
                combine(l)
            pe.wait_ge(xc_ready, sum(TOK_TILES))
            for tt in range(2):
                for k in range(KD):
                    last = turn(bank[(5, 6, 0, 7)[2 * tt + k // 4]][:, P * (k % 4):P * (k % 4) + P],
                                x_t[:, k, P * tt:P * tt + P], ident)
                last.then_inc(o_turned, 1)

        @block.scalar
        def _(act):
            do = nc.scalar.activation

            def norm_squares(n, width, arrived):
                for k in range(KD):
                    arrived(k)
                    if k >= 2:
                        act.wait_ge(sq_used, KD * n + k - 1)
                    do(sq[k % 2][:, 0:width], x_t[:, k, 0:width], ACT.Square).then_inc(sq_ready, 1)
                act.wait_ge(sq_used, KD * (n + 1))
                do(rstd[:, 0:width], bank[0][:, 0:width], ACT.Sqrt, bias=eps[:, 0:1]).then_inc(norm_root, 1)

            def norm_shift(n, width):
                l, w = divmod(n, 2)
                for k in range(KD):
                    act.wait_ge(hs_ready, KD * n + k + 1)
                    for src in range(width // 256):
                        m = l * NMOD + 3 * KD * w + k
                        cols = slice(256 * src, 256 * src + 256)
                        last = do(h_t[:, k, cols], h_t[:, k, cols], ACT.Identity, bias=mods[:, m, src:src + 1])
                    last.then_inc(h_ready, 1)

            def qkv(l):
                widths = [512, 512] + [P * TOK_TILES[l]] * 8

                def root(i):
                    act.wait_ge(qk_stats, 10 * l + i + 1)
                    if 10 * l + i > 0:
                        act.wait_ge(qk_done, 10 * l + i)
                    do(rstd[:, 0:widths[i]], bank[3][:, 0:widths[i]], ACT.Sqrt, bias=eps[:, 1:2]).then_inc(qk_root, 1)

                for i in range(10):
                    n = widths[i]
                    act.wait_ge(qk_mm, 10 * l + i + 1)
                    if i >= 2:
                        act.wait_ge(qk_stats, 10 * l + i - 1)
                    do(sq[i % 2][:, 0:n], bank[1 + i % 2][:, 0:n], ACT.Square)
                    kind = (1, 3)[i] if i < 2 else 2 * ((i - 2) // 4)
                    col = V_QN + DEPTH * kind + l
                    do(qk_t[:, i, 0:n], bank[1 + i % 2][:, 0:n], ACT.Identity,
                       scale=vec[:, col:col + 1]).then_inc(qk_evac, 1)
                    if i >= 1:
                        root(i - 1)
                root(9)
                for q in range(2):
                    act.wait_ge(v_mm, 2 * l + q + 1)
                    do(v_tok[:, 2 * q:2 * q + 2, :].rearrange("p t n -> p (t n)"), bank[5 + q][:, :],
                       ACT.Identity).then_inc(v_ready, 1)

            def attention(l):
                ub = sum(UNITS[:l])
                for n, (tt, T, kv, r) in enumerate(units(l)):
                    kn = keys(tt)[1]
                    head = l * 8 + 4 * kv + r
                    act.wait_ge(max_ready, ub + n + 1)
                    if n >= 4:
                        act.wait_ge(p_turned, ub + n - 3)
                    if T:
                        do(esink[:, n:n + 1], sink[:, head:head + 1], ACT.Exp, bias=negmax[:, n:n + 1])
                    do(probs[:, n % 4, 0:kn], bank[n % 3][:, 0:kn], ACT.Exp, bias=negmax[:, n:n + 1], scale=SCALE,
                       accum_out=lsum[:, n:n + 1]).then_inc(exp_done, 1)

            def y_tiles(l):
                act.wait_ge(zero_stored, 128)
                for m in range(0, KD, 2):
                    act.wait_ge(y_turned, KD * l + m + 1)
                    n = P * TOK_TILES[l]
                    do(h_t[:, m, 0:n], bank[1][:, 0:n], ACT.Identity).then_inc(yt_act, 1)

            def route(l):
                nt = TOK_TILES[l]
                act.wait_ge(lg_mm, l + 1)
                do(work[:, 512:512 + NE * nt], bank[1][:, 0:NE * nt], ACT.Sigmoid).then_inc(sig_ready, 1)
                for q in range(2 * nt):
                    act.wait_ge(h_turned, 2 * sum(TOK_TILES[:l]) + q + 1)
                    do(tokm[:, q // 2, 512 * (q % 2):512 * (q % 2) + 512], bank[2 + q % 4][:, :],
                       ACT.Identity).then_inc(tok_ready, 1)

            def experts(l):
                act.wait_ge(route_ready, l + 1)

                def rows_out(n):
                    act.wait_ge(rows_turned[l], n + 1)
                    act.wait_ge(rows_stored[l], 32 * n + 32)
                    do(yrow, bank[4][:, :], ACT.Identity).then_inc(rows_ready[l], 1)

                total = act.value_load(first[0:1, NE:NE + 1], min_val=1, max_val=MAX_CHUNKS[l])
                with act.Fori(0, total) as g:
                    act.wait_ge(gate_mm[l], g + 1)
                    do(act_g, bank[1][:, 0:256], ACT.Silu).then_inc(silu_done[l], 1)
                    rows_out(g)
                    act.wait_ge(down_mm[l], g + 1)
                    do(yc_t, bank[3][:, :], ACT.Identity).then_inc(yc_ready[l], 1)
                rows_out(total)

            def combine(l):
                for tt in range(TOK_TILES[l]):
                    act.wait_ge(yg_in[l][tt], 32)
                    do(ych[0][:, tt, :], ych[0][:, tt, :], ACT.Identity,
                       scale=wgt[:, tt:tt + 1]).then_inc(y_scaled, 1)

            act.dma_start(cst[:, :], table).then_inc(cst_in, 16)
            act.dma_start(vec_a, ada_b.rearrange("l (m p) -> (l m) p", p=P)).then_inc(vec_in, 16)

            def vec_rows(row, n, cols, src):
                r = row - 96
                act.dma_start(h_t[r:r + n, 0, P + cols[0]:P + cols[1]], src).then_inc(vec_in, 16)

            vec_rows(V_AG, DEPTH * KD, (0, P), attn_norm_g.rearrange("l (k p) -> (l k) p", p=P))
            vec_rows(V_FG, DEPTH * KD, (0, P), ffn_norm_g.rearrange("l (k p) -> (l k) p", p=P))
            vec_rows(V_C, KD, (0, P), c.rearrange("b (k p) -> (b k) p", p=P))
            vec_rows(V_CC, KD, (0, P), c_ctx.rearrange("(k p) -> k p", p=P))
            for i, g in enumerate((qn_global, kn_global, qn_local, kn_local)):
                for half in range(2):
                    vec_rows(V_QN + DEPTH * i, DEPTH, (HD * half, HD * half + HD), g)
            act.dma_start(tokm[:, 0:2, :], x[0].rearrange("(t p) d -> p t d", p=P)).then_inc(x_in, 16)
            act.dma_start(tokm[:, 2:4, :], ctx_in[0].rearrange("(t p) d -> p t d", p=P)).then_inc(x_in, 16)
            act.dma_start(sink[:, :], sink_logit.rearrange("l h -> (l h)").partition_broadcast(P)
                          ).then_inc(vec_in, 16)
            act.dma_start(rb[:, :], router_b.partition_broadcast(P)).then_inc(small_in, 16)
            act.dma_start(rw[:, :, :], router_w.rearrange("(k p) e -> p k e", p=P)).then_inc(small_in, 16)

            act.wait_ge(vec_ready, 1)
            do(scv[:, :, 0], vec[:, V_C:V_C + KD], ACT.Silu)
            do(scv[:, :, 1], vec[:, V_CC:V_CC + KD], ACT.Silu).then_inc(silu_ready, 1)
            for k in range(0, KD, 2):
                act.wait_ge(x_turned, k + 1)
                do(x_t[:, k, :], bank[1 + k % 6][:, :], ACT.Identity).then_inc(xt_act, 1)
            for l in range(DEPTH):
                if l == 0:
                    def arrived(k):
                        act.wait_ge((xt_act, xt_dve)[k % 2], k // 2 + 1)
                else:
                    def arrived(k):
                        act.wait_ge(xc_ready, TOK_TILES[0])
                norm_squares(2 * l, 512, arrived)
                norm_shift(2 * l, 512)
                qkv(l)
                attention(l)
                y_tiles(l)
                norm_squares(2 * l + 1, P * TOK_TILES[l], lambda k: act.wait_ge(xw_ready, KD * l + k + 1))
                norm_shift(2 * l + 1, P * TOK_TILES[l])
                route(l)
                experts(l)
                combine(l)
            for tt in range(2):
                act.wait_ge(o_turned, tt + 1)
                do(out_tok[:, tt, 0:512], bank[(5, 0)[tt]][:, :], ACT.Identity).then_inc(o_act, 1)

        @block.gpsimd
        def _(pool):
            def store_rows(l, g):
                for odd in range(2):
                    pool.dma_start(y_rows[bass.ds(g * CHUNK, CHUNK), 512 * odd:512 * odd + 512],
                                   yrow[CHUNK * odd:CHUNK * odd + CHUNK, :]).then_inc(rows_stored[l], 16)

            for l in range(DEPTH):
                nt = TOK_TILES[l]
                pool.wait_ge(qk_done, 10 * (l + 1))
                for T in range(2):
                    for a in range(2):
                        pool.dma_start(sq[T][HD * a:HD * a + HD, :], qk_t[HD * (1 - a):HD * (2 - a), T, :]
                                       ).then_inc(swapped, 16)
                if l == 0:
                    pool.wait_ge(zeros_set, 1)
                    for r in range((NE + 1) * CHUNK, y_rows.shape[0], P):
                        n = min(P, y_rows.shape[0] - r)
                        pool.dma_start(y_rows[r:r + n, :], zeros[0:n, :]).then_inc(zero_stored, 16)
                    pool.wait_ge(zero_stored, 128)
                else:
                    pool.wait_ge(xc_ready, sum(TOK_TILES[:l]))
                pool.wait_ge(route_ready, l + 1)
                pool.wait_ge(rows_ready[l], 1)
                store_rows(l, 0)
                total = pool.value_load(first[0:1, NE:NE + 1], min_val=1, max_val=MAX_CHUNKS[l])
                with pool.Fori(0, total) as g:
                    pool.wait_ge(rows_ready[l], g + 2)
                    store_rows(l, g)
                pool.wait_ge(rows_ready[l], total + 2)
                store_rows(l, total)
                pool.wait_ge(rows_stored[l], total * 32 + 64)
                pool.sem_inc(rows_all, 1)
                pool.wait_ge(rows_all, l + 1)
                pool.wait_ge(bufs_free, l + 1)
                for tt in range(nt):
                    for s in range(2):
                        pool.indirect_dma_start(ych[s][:, tt, :], None, y_rows[:, :],
                                                bass.IndirectOffsetOnAxis(posidx[:, nt * s + tt:nt * s + tt + 1], 0)
                                                ).then_inc(yg_in[l][tt], 16)

        @block.vector
        def _(dve):
            v = nc.vector
            chain = [0]

            def link(ins):
                chain[0] += 1
                ins.then_inc(dve_step, 1)
                dve.wait_ge(dve_step, chain[0])

            def gains(l):
                for w in range(2):
                    m = l * NMOD + (3 * w + 1) * KD
                    g0 = (V_AG, V_FG)[w] + l * KD
                    link(v.tensor_scalar(gain[:, l, w], mods[:, m:m + KD, :], 1.0, D ** 0.5, ALU.add, ALU.mult))
                    gv = vec[:, g0:g0 + KD].unsqueeze(2).to_broadcast([P, KD, 2])
                    link(v.tensor_tensor(gain[:, l, w], gain[:, l, w], gv, ALU.mult))

            def add_bias(m0, m1):
                ps = bank[7][:, 2 * m0:2 * m1].rearrange("p (m s) -> p m s", s=2)
                bias = vec[:, V_ADAB + m0:V_ADAB + m1].unsqueeze(2).to_broadcast([P, m1 - m0, 2])
                link(v.tensor_tensor(mods[:, m0:m1, :], ps, bias, ALU.add))

            def norm_scale(n, width):
                l, w = divmod(n, 2)
                dve.wait_ge(norm_root, n + 1)
                link(v.reciprocal(rstd[:, 0:width], rstd[:, 0:width]))
                for k in range(KD):
                    for src in range(width // 256):
                        cols = slice(256 * src, 256 * src + 256)
                        last = v.scalar_tensor_tensor(out=h_t[:, k, cols], in0=x_t[:, k, cols],
                                                      scalar=gain[:, l, w, k, src:src + 1], in1=rstd[:, cols],
                                                      op0=ALU.mult, op1=ALU.mult)
                    last.then_inc(hs_ready, 1)

            def qk_norms(l):
                widths = [512, 512] + [P * TOK_TILES[l]] * 8
                for i in range(10):
                    n = widths[i]
                    dve.wait_ge(qk_root, 10 * l + i + 1)
                    v.reciprocal(rstd[:, 0:n], rstd[:, 0:n])
                    v.tensor_tensor(rope_a, qk_t[:, i, 0:SEQ], cos, ALU.mult)
                    link(v.tensor_tensor(rope_b, bank[4][:, 0:SEQ], sin, ALU.mult))
                    link(v.tensor_tensor(qk_t[:, i, 0:SEQ], rope_a, rope_b, ALU.add))
                    v.scalar_tensor_tensor(out=qk_t[:, i, 0:n], in0=qk_t[:, i, 0:n], scalar=float(HD ** 0.5),
                                           in1=rstd[:, 0:n], op0=ALU.mult, op1=ALU.mult).then_inc(qk_done, 1)
                    dve.wait_ge(qk_done, 10 * l + i + 1)

            def attention(l):
                ub, gb = sum(UNITS[:l]), sum(UNITS[:l]) // 4
                us = units(l)
                nu = UNITS[l]
                dve.wait_ge(v_mm, 2 * (l + 1))
                if l == 0:
                    v.memset(zeros, 0.0)
                link(v.memset(esink[:, 0:nu], 0.0))
                dve.sem_inc(zeros_set, 1)

                def maxima(n):
                    tt, T, kv, r = us[n]
                    head = l * 8 + 4 * kv + r
                    dve.wait_ge(sc_done, ub + n + 1)
                    link(v.tensor_reduce(smx[:, n:n + 1], bank[n % 3][:, 0:keys(tt)[1]], AX.X, ALU.max))
                    if T:
                        ins = v.tensor_scalar(negmax[:, n:n + 1], smx[:, n:n + 1], -SCALE, nsink[:, head:head + 1],
                                              ALU.mult, ALU.min)
                    else:
                        ins = v.tensor_scalar(negmax[:, n:n + 1], smx[:, n:n + 1], -SCALE, None, ALU.mult)
                    ins.then_inc(max_ready, 1)

                def probs_out(n):
                    kn = keys(us[n][0])[1]
                    dve.wait_ge(p_turned, ub + n + 1)
                    if n >= 2:
                        dve.wait_ge(pv_done, ub + n - 1)
                    v.tensor_copy(probs_t[:, n % 2, 0:kn], bank[4 + n % 2][:, 0:kn]).then_inc(pt_ready, 1)

                def y_out(g):
                    tt, T, kv, _ = us[4 * g]
                    dve.wait_ge(pv_done, ub + 4 * g + 4)
                    link(v.tensor_tensor(ltot, lsum[:, 4 * g:4 * g + 4], esink[:, 4 * g:4 * g + 4], ALU.add))
                    link(v.reciprocal(lrec, ltot))
                    col = 512 * T + 256 * kv
                    v.tensor_tensor(tokm[:, tt, col:col + 256].rearrange("p (r d) -> p r d", r=4),
                                    bank[(3, 6)[g % 2]][:, 0:256].rearrange("p (r d) -> p r d", r=4),
                                    lrec.unsqueeze(2).to_broadcast([P, 4, HD]), ALU.mult).then_inc(y_evac, 1)

                for n in range(nu + 2):
                    if n < nu:
                        maxima(n)
                    if 2 <= n < nu + 2:
                        probs_out(n - 2)
                    if n >= 8 and n % 4 == 0:
                        y_out(n // 4 - 2)
                y_out(nu // 4 - 1)

            def y_tiles(l):
                dve.wait_ge(zero_stored, 128)
                for m in range(1, KD, 2):
                    dve.wait_ge(y_turned, KD * l + m + 1)
                    n = P * TOK_TILES[l]
                    v.tensor_copy(h_t[:, m, 0:n], bank[2][:, 0:n]).then_inc(yt_dve, 1)

            def add_attention(l):
                for m in range(KD):
                    dve.wait_ge(wo_mm, KD * l + m + 1)
                    for src in range(TOK_TILES[l] // 2):
                        cols = slice(256 * src, 256 * src + 256)
                        mod = l * NMOD + 2 * KD + m
                        last = v.scalar_tensor_tensor(out=x_t[:, m, cols], in0=bank[4 + m % 2][:, cols],
                                                      scalar=mods[:, mod, src:src + 1], in1=x_t[:, m, cols],
                                                      op0=ALU.mult, op1=ALU.add)
                    last.then_inc(xw_ready, 1)

            def route(l):
                nt = TOK_TILES[l]
                n16 = NE * nt

                def tmp(i):
                    return work[:, 64 * i:64 * i + n16]

                def te(a):
                    return a.rearrange("p (t e) -> p t e", t=nt)

                mask, eq, sel, oh1, oh2, cand, rank, pos = (tmp(i) for i in (0, 1, 2, 3, 4, 5, 6, 7))
                sc = work[:, 512:512 + n16]
                hi = work[:, 576:576 + 8 * nt]
                lo = work[:, 608:608 + 8 * nt]
                g4 = [work[:, 640 + 16 * i:640 + 16 * i + 4 * nt] for i in range(5)]
                t1 = [work[:, 720 + 4 * i:720 + 4 * i + nt] for i in range(4)]
                tot = work[:, 768:768 + NE]
                nch = work[:, 784:784 + NE]
                firstf = work[:, 800:800 + NE + 1]
                cmp = work[:, 832:832 + NE * (MAXCH - 1)]
                tri = work[:, 960:960 + NE * (NE + 1)]

                def per_tile(a, n):
                    return a.unsqueeze(2).to_broadcast([P, nt, n])

                def best(values, keys_, weights, n, hot, e4, c4):
                    link(v.tensor_reduce(t1[0], values, AX.X, ALU.max))
                    link(v.tensor_tensor(e4, values, per_tile(t1[0], n), ALU.is_equal))
                    link(v.tensor_tensor(c4, e4, weights.unsqueeze(1).to_broadcast([P, nt, n]), ALU.mult))
                    link(v.tensor_reduce(t1[0], c4, AX.X, ALU.max))
                    link(v.tensor_tensor(hot, c4, per_tile(t1[0], n), ALU.is_equal))

                dve.wait_ge(sig_ready, l + 1)
                if l == 0:
                    dve.wait_ge(small_in, 32)
                link(v.tensor_tensor(te(sel), te(sc), rb[:, :].unsqueeze(1).to_broadcast([P, nt, NE]), ALU.add))
                pair = sel.rearrange("p (g j i) -> p g j i", j=2, i=2)
                hi3 = hi.rearrange("p (g j) -> p g j", j=2)
                lo3 = lo.rearrange("p (g j) -> p g j", j=2)
                v.tensor_tensor(hi3, pair[:, :, :, 0], pair[:, :, :, 1], ALU.max)
                link(v.tensor_tensor(lo3, pair[:, :, :, 0], pair[:, :, :, 1], ALU.min))
                v.tensor_tensor(g4[0], hi3[:, :, 0], hi3[:, :, 1], ALU.max)
                v.tensor_tensor(g4[1], hi3[:, :, 0], hi3[:, :, 1], ALU.min)
                link(v.tensor_tensor(g4[2], lo3[:, :, 0], lo3[:, :, 1], ALU.max))
                link(v.tensor_tensor(g4[1], g4[1], g4[2], ALU.max))
                link(v.tensor_tensor(g4[0], g4[0], g4[1], ALU.add))
                tg = [a.rearrange("p (t g) -> p t g", t=nt) for a in g4]
                best(tg[0], None, cst[:, C_W4:C_W4 + NG], NG, tg[3], tg[1], tg[2])
                link(v.tensor_scalar(g4[4], g4[3], 1.0, BIG, ALU.subtract, ALU.mult))
                link(v.tensor_tensor(sel.rearrange("p (g i) -> p g i", i=EPG), sel.rearrange("p (g i) -> p g i", i=EPG),
                                     g4[4].unsqueeze(2).to_broadcast([P, NG * nt, EPG]), ALU.add))
                best(te(sel), None, cst[:, C_W16:C_W16 + NE], NE, te(oh1), te(eq), te(cand))
                link(v.scalar_tensor_tensor(out=sel, in0=oh1, scalar=-3e38, in1=sel, op0=ALU.mult, op1=ALU.add))
                best(te(sel), None, cst[:, C_W16:C_W16 + NE], NE, te(oh2), te(eq), te(cand))
                v.tensor_tensor(mask, oh1, oh2, ALU.add).then_inc(mask_ready, 1)
                for s, oh in enumerate((oh1, oh2)):
                    link(v.tensor_tensor(eq, oh, sc, ALU.mult))
                    link(v.tensor_reduce(t1[1 + s], te(eq), AX.X, ALU.add))
                link(v.tensor_tensor(t1[3], t1[1], t1[2], ALU.add))
                link(v.reciprocal(t1[3], t1[3]))
                v.tensor_tensor(wgt[:, 0:nt], t1[1], t1[3], ALU.mult)
                v.tensor_tensor(wgt[:, nt:2 * nt], t1[2], t1[3], ALU.mult)
                dve.wait_ge(rank_mm, l + 1)
                v.tensor_copy(rank, bank[6][:, 0:n16])
                link(v.tensor_copy(tot, bank[6][:, n16:n16 + NE]))
                link(v.tensor_tensor(cmp.rearrange("p (e j) -> p e j", e=NE), tot.unsqueeze(2).to_broadcast([P, NE, MAXCH - 1]),
                                     cst[:, C_THR:C_W16].unsqueeze(1).to_broadcast([P, NE, MAXCH - 1]), ALU.is_gt))
                link(v.tensor_reduce(nch, cmp.rearrange("p (e j) -> p e j", e=NE), AX.X, ALU.add))
                link(v.tensor_scalar(nch, nch, 1.0, None, ALU.add))
                link(v.tensor_tensor(tri.rearrange("p (f e) -> p f e", e=NE), nch.unsqueeze(1).to_broadcast([P, NE + 1, NE]),
                                     cst[:, C_TRI:C_THR].rearrange("p (f e) -> p f e", e=NE), ALU.mult))
                link(v.tensor_reduce(firstf, tri.rearrange("p (f e) -> p f e", e=NE), AX.X, ALU.add))
                v.tensor_copy(first[:, :], firstf)
                link(v.scalar_tensor_tensor(out=te(pos), in0=firstf[:, 0:NE].unsqueeze(1).to_broadcast([P, nt, NE]),
                                            scalar=float(CHUNK), in1=te(rank), op0=ALU.mult, op1=ALU.add))
                for s, oh in enumerate((oh1, oh2)):
                    link(v.tensor_tensor(eq, oh, pos, ALU.mult))
                    link(v.tensor_reduce(posrel[:, nt * s:nt * s + nt], te(eq), AX.X, ALU.add))
                link(v.tensor_scalar(posidx[:, 0:2 * nt], posrel[:, 0:2 * nt], float(CHUNK), None, ALU.add))
                v.memset(yc_t, 0.0).then_inc(yc_ready[l], 1)
                v.memset(yrow, 0.0).then_inc(rows_ready[l], 1)
                dve.sem_inc(route_ready, 1)

            def experts(l):
                nt = TOK_TILES[l]

                def build_pick(n):
                    pk2 = pick2[:, 0:2 * nt * CHUNK]
                    loop = loop_step[l]
                    v.tensor_tensor(pk2.rearrange("p (s c) -> p s c", c=CHUNK),
                                    iota.unsqueeze(1).to_broadcast([P, 2 * nt, CHUNK]),
                                    posrel[:, 0:2 * nt].unsqueeze(2).to_broadcast([P, 2 * nt, CHUNK]),
                                    ALU.is_equal).then_inc(loop, 1)
                    dve.wait_ge(loop, 2 * n + 1)
                    v.tensor_tensor(pick[:, 0:nt * CHUNK], pk2[:, 0:nt * CHUNK], pk2[:, nt * CHUNK:2 * nt * CHUNK],
                                    ALU.add).then_inc(pick_ready[l], 1)
                    v.tensor_scalar(posrel[:, 0:2 * nt], posrel[:, 0:2 * nt], -float(CHUNK), None,
                                    ALU.add).then_inc(loop, 1)
                    dve.wait_ge(loop, 2 * n + 2)

                def chunk_out(n):
                    dve.wait_ge(gather_mm[l], n + 1)
                    v.tensor_copy(hc_t, bank[0][:, :]).then_inc(hc_ready[l], 1)

                total = dve.value_load(first[0:1, NE:NE + 1], min_val=1, max_val=MAX_CHUNKS[l])
                build_pick(0)
                chunk_out(0)
                with dve.Fori(0, total) as g:
                    build_pick(g + 1)
                    dve.wait_ge(silu_done[l], g + 1)
                    dve.wait_ge(up_mm[l], g + 1)
                    v.tensor_tensor(he_t, bank[2][:, 0:256], act_g, ALU.mult).then_inc(he_ready[l], 1)
                    chunk_out(g + 1)
                dve.wait_ge(hc_ready[l], total + 1)
                dve.sem_inc(bufs_free, 1)

            def combine(l):
                nt = TOK_TILES[l]
                tb = sum(TOK_TILES[:l])

                def add_rows(tt):
                    dve.wait_ge(c_turned, tb + tt + 1)
                    for k in range(KD):
                        mod = l * NMOD + 5 * KD + k
                        ps = bank[1 + 2 * (tt % 2) + k // 4][:, P * (k % 4):P * (k % 4) + P]
                        xs = x_t[:, k, P * tt:P * tt + P]
                        last = v.scalar_tensor_tensor(out=xs, in0=ps, scalar=mods[:, mod, tt // 2:tt // 2 + 1],
                                                      in1=xs, op0=ALU.mult, op1=ALU.add)
                    last.then_inc(xc_ready, 1)

                for tt in range(nt):
                    dve.wait_ge(y_scaled, tb + tt + 1)
                    v.scalar_tensor_tensor(out=ych[0][:, tt, :], in0=ych[1][:, tt, :],
                                           scalar=wgt[:, nt + tt:nt + tt + 1], in1=ych[0][:, tt, :],
                                           op0=ALU.mult, op1=ALU.add).then_inc(y_summed, 1)
                    if tt >= 1:
                        add_rows(tt - 1)
                add_rows(nt - 1)

            v.memset(eps[:, 0:1], D * EPS)
            v.memset(eps[:, 1:2], HD * EPS)
            v.memset(ones[:, :], 1.0).then_inc(ones_set, 1)
            dve.wait_ge(vec_turned, 1)
            v.tensor_copy(vec[:, :], bank[0][:, 0:V_END]).then_inc(vec_ready, 1)
            dve.wait_ge(vec_in, 16 * 14)
            link(v.tensor_scalar(nsink[:, :], sink[:, :], -1.0, None, ALU.mult))
            for k in range(1, KD, 2):
                dve.wait_ge(x_turned, k + 1)
                v.tensor_copy(x_t[:, k, :], bank[1 + k % 6][:, :]).then_inc(xt_dve, 1)
            dve.wait_ge(ada_used, 4)
            add_bias(0, 2 * KD)
            link(v.tensor_scalar(gain[:, 0, 0], mods[:, KD:2 * KD, :], 1.0, D ** 0.5, ALU.add, ALU.mult))
            link(v.tensor_tensor(gain[:, 0, 0], gain[:, 0, 0],
                                 vec[:, V_AG:V_AG + KD].unsqueeze(2).to_broadcast([P, KD, 2]), ALU.mult))
            dve.sem_inc(mods_ready, 1)
            for l in range(DEPTH):
                norm_scale(2 * l, 512)
                qk_norms(l)
                attention(l)
                y_tiles(l)
                if l == 0:
                    dve.wait_ge(ada_used, 24)
                    add_bias(2 * KD, DEPTH * NMOD)
                    gains(0)
                    gains(1)
                    dve.sem_inc(mods_ready, 1)
                add_attention(l)
                norm_scale(2 * l + 1, P * TOK_TILES[l])
                route(l)
                experts(l)
                combine(l)
            for tt in range(2):
                dve.wait_ge(o_turned, tt + 1)
                v.tensor_copy(out_tok[:, tt, 512:D], bank[(6, 7)[tt]][:, :]).then_inc(o_dve, 1)


_INS = ['x', 'c', 'ctx', 'c_ctx', 'ada_w', 'ada_b', 'attn_norm_g', 'ffn_norm_g', 'w_in', 'qn_global', 'kn_global',
        'qn_local', 'kn_local', 'sink_logit', 'w_out', 'router_w', 'router_b', 'w_gate', 'w_up', 'w_down']


def kernel(**inputs):
    import numpy as _np
    import concourse.bacc as _bacc
    from concourse import mybir as _mybir
    from concourse.bass_utils import run_bass_kernel_spmd as _run

    nc = _bacc.Bacc("TRN2", target_bir_lowering=False, num_devices=1)
    arrays, args = {}, []
    for name in _INS:
        a = _np.ascontiguousarray(inputs[name])
        arrays[f"in_{name}_dram"] = a
        args.append(nc.dram_tensor(f"in_{name}_dram", a.shape, _mybir.dt.from_np(a.dtype), kind="ExternalInput").ap())
    a = constants()
    arrays["in_table_dram"] = a
    args.append(nc.dram_tensor("in_table_dram", a.shape, _mybir.dt.from_np(a.dtype), kind="ExternalInput").ap())
    out = nc.dram_tensor("out_dram", (1, SEQ, D), F32, kind="ExternalOutput").ap()
    backbone(nc, *args, out)
    r = _run(nc, [arrays], core_ids=[0])
    return r.results[0]["out_dram"]
```

```python
from contextlib import ExitStack

import concourse.bass as bass
from concourse import mybir

F32 = mybir.dt.float32
I32 = mybir.dt.int32
BF16 = mybir.dt.bfloat16
U32 = mybir.dt.uint32
ALU = mybir.AluOpType
ACT = mybir.ActivationFunctionType
AX = mybir.AxisListType

P = 128
D = 1024
KD = D // P
SEQ = 256
CTX = 256
DEPTH = 2
HD = 64
IN_W = 1536
NE = 16
NG = 4
EPG = NE // NG
FE = 512
KF = FE // P
NMOD = 6 * KD
EPS = 1e-6
SCALE = HD ** -0.5
NEG = -1e30
CHUNK = 128
MAXCH = 512 // CHUNK
BIG = 1e30

TOK_TILES = [(SEQ + CTX) // P, SEQ // P]
UNITS = [16 * t for t in TOK_TILES]
MAX_CHUNKS = [NE + 2 * t * P // CHUNK for t in TOK_TILES]
GT = max(MAX_CHUNKS) + 2
ROWS = 2 * (SEQ + CTX)

C_ID, C_BLK, C_SWP = 0, P, 2 * P
C_COS = 3 * P
C_SIN = C_COS + SEQ
C_M0 = C_SIN + SEQ
C_M1 = C_M0 + P
C_G = C_M1 + P
C_TRI = C_G + GT
C_THR = C_TRI + (NE + 1) * NE
C_W16 = C_THR + MAXCH - 1
C_W4 = C_W16 + NE
C_END = C_W4 + NG
C_UP = C_END
C_ALL = C_UP + P

V_ADAB = 0
V_AG = DEPTH * NMOD
V_FG = V_AG + DEPTH * KD
V_C = V_FG + DEPTH * KD
V_CC = V_C + KD
V_QN = V_CC + KD
V_END = V_QN + 4 * DEPTH


def constants():
    import numpy as np
    t = np.zeros((P, C_ALL), np.float32)
    i = np.arange(P)
    t[:, C_ID:C_ID + P] = np.eye(P)
    t[:, C_UP:C_UP + P] = i[:, None] < i[None, :]
    t[:, C_BLK:C_BLK + P] = i[:, None] // HD == i[None, :] // HD
    t[:, C_SWP:C_SWP + P] = (i[:, None] ^ 16) == i[None, :]
    tok = np.arange(SEQ)
    grid = np.stack([tok // 64, tok % 64]).astype(np.float32)
    nf = HD // 4
    inv = np.float32(10000.0) ** (-np.arange(nf, dtype=np.float32) / np.float32(nf))
    d = i % HD
    ang = (grid[d // 32] * inv[d % nf][:, None]).astype(np.float32)
    t[:, C_COS:C_COS + SEQ] = np.cos(ang)
    t[:, C_SIN:C_SIN + SEQ] = np.where((d % 32 < 16)[:, None], -np.sin(ang), np.sin(ang))
    t[:, C_M0:C_M0 + P] = np.where(i[None, :] > i[:, None], NEG, 0.0)
    t[:, C_M1:C_M1 + P] = np.where(i[None, :] < i[:, None], NEG, 0.0)
    t[:, C_G:C_G + GT] = np.arange(GT)
    e = np.arange(NE)
    t[:, C_TRI:C_THR] = (e[None, :] < np.arange(NE + 1)[:, None]).reshape(-1)
    t[:, C_THR:C_W16] = CHUNK * np.arange(1, MAXCH)
    t[:, C_W16:C_W4] = NE - e
    t[:, C_W4:C_END] = NG - np.arange(NG)
    return t


def backbone(nc, x, c, ctx_in, c_ctx, ada_w, ada_b, attn_norm_g, ffn_norm_g, w_in, qn_global, kn_global,
             qn_local, kn_local, sink_logit, w_out, router_w, router_b, w_gate, w_up, w_down, table, out):
    with ExitStack() as stack:
        def sb(name, shape, dt=F32):
            return stack.enter_context(nc.sbuf_tensor(name, shape, dt))

        def sem(name):
            return stack.enter_context(nc.semaphore(name))

        def per_layer(name):
            return [sem(f"{name}{l}") for l in range(DEPTH)]

        ring = sb("ring", [P, 9, 4096])
        x_t = sb("x_t", [P, KD, 512])
        h_t = sb("h_t", [P, KD, 512])
        tokm = sb("tokm", [P, 4, D])
        cst = sb("cst", [P, C_END])
        ones = sb("ones", [P, P])
        eps = sb("eps", [P, 2])
        rw = sb("rw", [P, KD, NE])
        rb = sb("rb", [P, NE])
        sink = sb("sink", [P, DEPTH * 8])
        nsink = sb("nsink", [P, DEPTH * 8])
        work = sb("work", [P, 1536])
        vec = sb("vec", [P, V_END])
        scv = sb("scv", [P, KD, 2])
        mods = sb("mods", [P, DEPTH * NMOD, 2])
        gain = sb("gain", [P, DEPTH, 2, KD, 2])
        upper_b = sb("upper_b", [P, P], BF16)
        ones_b = sb("ones_b", [P, P], BF16)
        mask_b = sb("mask_b", [P, 64], BF16)
        pos = sb("pos", [P, 8])
        posidx = sb("posidx", [P, 8], U32)
        wgt = sb("wgt", [P, 8])
        first = sb("first", [P, NE + 1], I32)
        chunk_row = sb("chunk_row", [P, GT], I32)

        bank = [stack.enter_context(nc.psum_tensor(f"bank{i}", [P, 512], F32)) for i in range(8)]
        h_rows = nc.dram_tensor("h_rows", [ROWS + CHUNK, D], F32, kind="Internal").ap()
        y_rows = nc.dram_tensor("y_rows", [ROWS + CHUNK, D], F32, kind="Internal").ap()

        ident = cst[:, C_ID:C_ID + P]
        head_ones = cst[:, C_BLK:C_BLK + P]
        swap = cst[:, C_SWP:C_SWP + P]
        cos = cst[:, C_COS:C_COS + SEQ]
        sin = cst[:, C_SIN:C_SIN + SEQ]
        band = [cst[:, C_M0:C_M0 + P], cst[:, C_M1:C_M1 + P]]
        upper_f = h_t[:, 0, 2 * P:3 * P]

        vec_a = h_t[0:96, 0, 0:P]
        vec_b = h_t[0:V_END - 96, 0, P:2 * P]
        sq = [work[:, 0:512], work[:, 512:1024]]
        rstd = work[:, 1024:1536]
        win = ring[:, 3:6, :].rearrange("p a b -> p (a b)").rearrange("p (k n) -> p k n", k=KD)
        wout = [ring[:, 6, :].rearrange("p (k n) -> p k n", k=4), ring[:, 3, :].rearrange("p (k n) -> p k n", k=4)]
        scratch = ring[:, 7:9, :].rearrange("p a b -> p (a b)")
        qk_t = scratch[:, 0:5120].rearrange("p (i n) -> p i n", i=10)
        v_tok = scratch[:, 5120:6144].rearrange("p (t n) -> p t n", t=4)
        probs = scratch[:, 6144:8192].rearrange("p (b n) -> p b n", b=4)
        rope_a = probs[:, 0, 0:SEQ]
        rope_b = probs[:, 1, 0:SEQ]
        probs_t = h_t[:, 0:4, :]
        parts = h_t[:, 5, :]
        y_t = tokm[:, :, :].rearrange("p t n -> p (t n)").rearrange("p (k n) -> p k n", k=KD)
        smx = h_t[:, 4, 0:64]
        negmax = h_t[:, 4, 64:128]
        lsum = h_t[:, 4, 128:192]
        esink = h_t[:, 4, 192:256]
        lrec = h_t[:, 4, 256:320]
        hflat = h_t[:, :, :].rearrange("p k n -> p (k n)")
        hc = hflat[:, 0:1024]
        hc_t = hflat[:, 1024:2048].rearrange("p (k t) -> p k t", k=KD)
        act_g = hflat[:, 2048:2560]
        he = hflat[:, 2560:3072]
        he_t = hflat[:, 3072:3584].rearrange("p (k t) -> p k t", k=KF)
        yrow = work[:, 0:1024]
        ych = [tokm, hflat.rearrange("p (t n) -> p t n", t=4)]
        out_tok = ring[:, 0:1, :].rearrange("p a b -> p (a b)")[:, 0:2 * D].rearrange("p (t n) -> p t n", t=2)

        cst_in, vec_in, x_in, small_in = sem("cst_in"), sem("vec_in"), sem("x_in"), sem("small_in")
        ada_in = [sem(f"ada_in{s}") for s in range(4)]
        ada2_in = [sem(f"ada2_in{s}") for s in range(4)]
        win_in = [sem(f"win_in{s}") for s in range(4)]
        wout_in = [sem(f"wout_in{s}") for s in range(2)]
        ew_in = [[sem(f"ew_in{l}_{s}") for s in range(9)] for l in range(DEPTH)]
        set_free = [[sem(f"set_free{l}_{s}") for s in range(3)] for l in range(DEPTH)]
        ones_set = sem("ones_set")
        vec_turned, vec_ready, silu_ready = sem("vec_turned"), sem("vec_ready"), sem("silu_ready")
        x_turned, xt_act, xt_dve = sem("x_turned"), sem("xt_act"), sem("xt_dve")
        ada_used, mods_ready = sem("ada_used"), sem("mods_ready")
        bank7_set, parts_ready, ada_turned, ada_summed = (sem(n) for n in ("bank7_set", "parts_ready", "ada_turned",
                                                                           "ada_summed"))
        sq_ready, sq_used, hs_ready, h_ready = sem("sq_ready"), sem("sq_used"), sem("hs_ready"), sem("h_ready")
        norm_root, qk_root = sem("norm_root"), sem("qk_root")
        qk_mm, qk_evac, qk_stats, qk_done = sem("qk_mm"), sem("qk_evac"), sem("qk_stats"), sem("qk_done")
        v_mm, v_ready, swapped = sem("v_mm"), sem("v_ready"), sem("swapped")
        p_scaled = sem("p_scaled")
        sc_done, max_ready, exp_done = sem("sc_done"), sem("max_ready"), sem("exp_done")
        p_turned, pt_ready, pv_done, y_evac = sem("p_turned"), sem("pt_ready"), sem("pv_done"), sem("y_evac")
        wo_mm, xw_ready = sem("wo_mm"), sem("xw_ready")
        lg_mm, sig_ready, h_turned, tok_ready = sem("lg_mm"), sem("sig_ready"), sem("h_turned"), sem("tok_ready")
        mask_ready, rank_mm, route_ready = sem("mask_ready"), sem("rank_mm"), sem("route_ready")
        hc_in, hc_turned, hc_ready = per_layer("hc_in"), per_layer("hc_turned"), per_layer("hc_ready")
        gu_mm, silu_done, he_ready = per_layer("gu_mm"), per_layer("silu_done"), per_layer("he_ready")
        he_turned, het_ready, down_mm = per_layer("he_turned"), per_layer("het_ready"), per_layer("down_mm")
        rows_ready, rows_stored = per_layer("rows_ready"), per_layer("rows_stored")
        scattered, rows_all, esink_set = sem("scattered"), sem("rows_all"), sem("esink_set")
        yg_in = [[sem(f"yg_in{l}_{t}") for t in range(4)] for l in range(DEPTH)]
        y_scaled, y_summed, c_turned, xc_ready = sem("y_scaled"), sem("y_summed"), sem("c_turned"), sem("xc_ready")
        o_turned, o_act, o_dve, out_done = sem("o_turned"), sem("o_act"), sem("o_dve"), sem("out_done")
        dve_step = sem("dve_step")

        def units(l):
            return [(tt, T, kv, r) for tt in range(TOK_TILES[l]) for T in range(2) for kv in range(2)
                    for r in range(4)]

        def keys(tt):
            return (0, 512) if tt < 2 else (256, 256)

        def expert_weights(e, a):
            return [(3 * a, w_gate, KD), (3 * a + 1, w_up, KD), (3 * a + 2, w_down, KF)]

        block = stack.enter_context(nc.Block())

        @block.sync
        def _(sp):
            def slot(s, k):
                return ring[:, s, :].rearrange("p (k n) -> p k n", k=k)

            def load_ada(s, u, signal):
                l, m = divmod(u, 12)
                sp.dma_start(slot(s, KD), ada_w[l, :, m * 512:m * 512 + 512].rearrange("(k p) n -> p k n", p=P)
                             ).then_inc(signal, 16)

            def load_win(l):
                for q in range(4):
                    sp.dma_start(win[:, 2 * q:2 * q + 2, :],
                                 w_in[l, 256 * q:256 * q + 256, :].rearrange("(k p) n -> p k n", p=P)
                                 ).then_inc(win_in[q], 16)

            def load_wout(l, half):
                sp.dma_start(wout[half], w_out[l, 512 * half:512 * half + 512, :].rearrange("(k p) n -> p k n", p=P)
                             ).then_inc(wout_in[half], 16)

            def load_expert(l, e, a, parts=(0, 1, 2)):
                for part in parts:
                    s, w, k = expert_weights(e, a)[part]
                    src = w[l, bass.ds(e, 1)].rearrange("a (k p) n -> p (a k) n", p=P)
                    sp.dma_start(slot(s, k), src).then_inc(ew_in[l][s], 16)

            sp.dma_start(cst[:, :], table[:, 0:C_END]).then_inc(cst_in, 16)
            sp.dma_start(tokm[:, 0:2, :], x[0].rearrange("(t p) d -> p t d", p=P)).then_inc(x_in, 16)
            sp.dma_start(tokm[:, 2:4, :], ctx_in[0].rearrange("(t p) d -> p t d", p=P)).then_inc(x_in, 16)
            sp.wait_ge(vec_in, 16 * 15)
            for u, s in enumerate((6, 0, 1, 2)):
                load_ada(s, u, ada_in[u])
            load_win(0)
            for part in range(3):
                sp.wait_ge(ada_used, part + 2)
                load_expert(0, 0, 0, (part,))
            for u in range(4, 24):
                if u == 5:
                    sp.wait_ge(v_mm, 2)
                if u >= 8:
                    sp.wait_ge(ada_used, u - 3)
                load_ada((6, 3, 4, 5)[u % 4], u, ada2_in[u % 4])
            for l in range(DEPTH):
                if l == 0:
                    sp.wait_ge(ada_used, 21)
                    load_wout(0, 0)
                    sp.wait_ge(ada_used, 22)
                    load_wout(0, 1)
                    sp.wait_ge(ada_used, 24)
                else:
                    sp.wait_ge(set_free[0][1], 5)
                    load_win(1)
                    sp.wait_ge(set_free[0][2], 5)
                    load_wout(1, 0)
                    sp.wait_ge(set_free[0][0], 6)
                    load_expert(1, 0, 0)
                    sp.wait_ge(v_mm, 4)
                    load_wout(1, 1)
                load_expert(l, 1, 1, (1, 2))
                sp.wait_ge(pv_done, sum(UNITS[:l + 1]) // 4)
                load_expert(l, 2, 2, (1, 2))
                sp.wait_ge(wo_mm, KD * (l + 1))
                load_expert(l, 1, 1, (0,))
                load_expert(l, 2, 2, (0,))
                with sp.Fori(1, 5) as i:
                    for a in range(3):
                        sp.wait_ge(set_free[l][a], i)
                        load_expert(l, 3 * i + a, a)
                sp.wait_ge(set_free[l][0], 5)
                load_expert(l, 15, 0)
            for tt in range(2):
                sp.wait_ge(o_act, tt + 1)
                sp.wait_ge(o_dve, tt + 1)
                sp.dma_start(out[0, P * tt:P * tt + P, :], out_tok[:, tt, :]).then_inc(out_done, 16)
            sp.wait_ge(out_done, 32)

        @block.tensor
        def _(pe):
            mm = nc.tensor.matmul
            turn = nc.tensor.transpose

            def ada_unit(u):
                if u < 4:
                    s = (6, 0, 1, 2)[u]
                    pe.wait_ge(ada_in[u], 16)
                else:
                    s = (6, 3, 4, 5)[u % 4]
                    pe.wait_ge(ada2_in[u % 4], 16 * (u // 4))
                if u > 0:
                    pe.wait_ge(parts_ready, u)
                w = ring[:, s, :].rearrange("p (k n) -> p k n", k=KD)
                for k in range(KD):
                    q = k % 4
                    last = mm(bank[7][32 * q:32 * q + 2, :], scv[:, k, :], w[:, k, :],
                              start=(k < 4), stop=(k >= 4))
                last.then_inc(ada_used, 1)

            def ada_turn(u):
                pe.wait_ge(parts_ready, u + 1)
                if u > 0:
                    pe.wait_ge(ada_summed, u)
                for m in range(4):
                    last = turn(bank[2][:, P * m:P * m + P], parts[:, P * m:P * m + P], ident)
                last.then_inc(ada_turned, 1)

            def norm_sums(n, width):
                for k in range(KD):
                    pe.wait_ge(sq_ready, KD * n + k + 1)
                    mm(bank[0][:, 0:width], ones[:, :], sq[k % 2][:, 0:width],
                       start=(k == 0), stop=(k == KD - 1)).then_inc(sq_used, 1)

            def qk_weights(i, k):
                T, j = divmod(i - 2, 4)
                col = 512 + 768 * i if i < 2 else 768 * T + P * j
                return win[:, k, col:col + P]

            def qk_sums(l, i, n):
                pe.wait_ge(qk_evac, 10 * l + i + 1)
                if 10 * l + i > 0:
                    pe.wait_ge(qk_done, 10 * l + i)
                mm(bank[3][:, 0:n], head_ones, sq[i % 2][:, 0:n], start=True, stop=True)
                mm(bank[4][:, 0:SEQ], swap, qk_t[:, i, 0:SEQ], start=True, stop=True).then_inc(qk_stats, 1)

            def qkv(l):
                widths = [512, 512] + [P * TOK_TILES[l]] * 8
                for i in range(10):
                    if i >= 2:
                        pe.wait_ge(qk_evac, 10 * l + i - 1)
                    for k in range(KD):
                        if i == 0:
                            pe.wait_ge(h_ready, 2 * KD * l + k + 1)
                            pe.wait_ge(win_in[k // 2], 16 * (l + 1))
                        last = mm(bank[1 + i % 2][:, 0:widths[i]], qk_weights(i, k), h_t[:, k, 0:widths[i]],
                                  start=(k == 0), stop=(k == KD - 1))
                    last.then_inc(qk_mm, 1)
                    if i >= 1:
                        qk_sums(l, i - 1, widths[i - 1])
                for tt in range(4):
                    for k in range(KD):
                        wv = win[:, k, :].rearrange("p (h n) -> p h n", h=2)[:, :, 640:768]
                        o = bank[5 + tt // 2][:, 256 * (tt % 2):256 * (tt % 2) + 256].rearrange("p (h n) -> p h n", h=2)
                        last = mm(o, h_t[:, k, P * tt:P * tt + P], wv, start=(k == 0), stop=(k == KD - 1))
                    if tt % 2:
                        last.then_inc(v_mm, 1)
                    if tt == 0:
                        qk_sums(l, 9, widths[9])

            def attention(l):
                ub, gb = sum(UNITS[:l]), sum(UNITS[:l]) // 4
                us = units(l)

                def scores(n):
                    tt, T, kv, r = us[n]
                    k0, kn = keys(tt)
                    if n == 0:
                        pe.wait_ge(qk_done, 10 * (l + 1))
                        pe.wait_ge(swapped, 64 * (l + 1))
                    if n >= 2:
                        pe.wait_ge(exp_done, ub + n - 1)
                    a = r % 2
                    rows = slice(HD * a, HD * a + HD)
                    k_t = (qk_t[:, T] if a == kv else sq[T])[rows, k0:k0 + kn]
                    q_t = qk_t[rows, 2 + 4 * T + 2 * kv + r // 2, P * tt:P * tt + P]
                    o = bank[n % 2]
                    parts = [(0, kn, False)]
                    if T == 1 and tt < 2:
                        parts = ([(0, P, False), (P, 2 * P, True), (2 * P, kn, False)] if tt == 0 else
                                 [(0, P, True), (P, kn, False)])
                    for c0, c1, masked in parts:
                        last = mm(o[:, c0:c1], q_t, k_t[:, c0:c1], start=True, stop=not masked)
                        if masked:
                            last = mm(o[:, c0:c1], ident, band[tt], start=False, stop=True)
                    last.then_inc(sc_done, 1)

                def turn_probs(n):
                    tt = us[n][0]
                    pe.wait_ge(p_scaled, ub + n + 1)
                    if n >= 2:
                        pe.wait_ge(pt_ready, ub + n - 1)
                    for q in range(keys(tt)[1] // P):
                        last = turn(bank[4 + n % 2][:, P * q:P * q + P], probs[:, n % 4, P * q:P * q + P], ident)
                    last.then_inc(p_turned, 1)

                def values(g):
                    tt, T, kv, _ = us[4 * g]
                    k0, kn = keys(tt)
                    pe.wait_ge(pt_ready, ub + 4 * g + 4)
                    if g == 0:
                        pe.wait_ge(v_ready, 2 * (l + 1))
                    if g >= 2:
                        pe.wait_ge(y_evac, gb + g - 1)
                    nk = kn // P
                    col = P * T + HD * kv
                    for q in range(nk):
                        for odd in range(2):
                            last = mm(bank[(3, 6)[g % 2]][HD * odd:HD * odd + HD, 0:256],
                                      v_tok[:, k0 // P + q, col:col + HD],
                                      probs_t[:, q, 256 * odd:256 * odd + 256], start=(q == 0), stop=(q == nk - 1))
                    last.then_inc(pv_done, 1)

                for n in range(UNITS[l] + 4):
                    if n < UNITS[l]:
                        scores(n)
                    if n >= 6 and n % 4 == 2:
                        values(n // 4 - 1)
                    if 2 <= n < UNITS[l] + 2:
                        turn_probs(n - 2)
                    if l == 0 and n % 3 == 1 and n // 3 < 20:
                        ada_unit(4 + n // 3)
                    if l == 0 and n % 3 == 2 and n // 3 < 20:
                        ada_turn(4 + n // 3)

            def project_out(l):
                nt = TOK_TILES[l]
                pe.wait_ge(y_evac, sum(UNITS[:l + 1]) // 4)
                for m in range(KD):
                    if m >= 2:
                        pe.wait_ge(xw_ready, KD * l + m - 1)
                    for k in range(KD):
                        if m == 0:
                            pe.wait_ge(wout_in[k // 4], 16 * (l + 1))
                        last = mm(bank[4 + m % 2][:, 0:P * nt], wout[k // 4][:, k % 4, P * m:P * m + P],
                                  y_t[:, k, 0:P * nt], start=(k == 0), stop=(k == KD - 1))
                    last.then_inc(wo_mm, 1)

            def route(l):
                nt = TOK_TILES[l]
                tb = 2 * sum(TOK_TILES[:l])
                for tt in range(nt):
                    for k in range(KD):
                        if tt == 0:
                            pe.wait_ge(h_ready, KD * (2 * l + 1) + k + 1)
                        last = mm(bank[1][:, NE * tt:NE * tt + NE], h_t[:, k, P * tt:P * tt + P], rw[:, k, :],
                                  start=(k == 0), stop=(k == KD - 1))
                last.then_inc(lg_mm, 1)
                for q in range(2 * nt):
                    if q >= 4:
                        pe.wait_ge(tok_ready, tb + q - 3)
                    for k in range(4):
                        kk = 4 * (q % 2) + k
                        last = turn(bank[2 + q % 4][:, P * k:P * k + P], h_t[:, kk, P * (q // 2):P * (q // 2) + P], ident)
                    last.then_inc(h_turned, 1)
                pe.wait_ge(mask_ready, l + 1)
                mask = mask_b[:, 0:NE * nt].rearrange("p (t e) -> p t e", t=nt)
                for tt in range(nt):
                    for t2 in range(tt + 1):
                        mm(bank[6][:, NE * tt:NE * tt + NE], upper_b[:, :] if t2 == tt else ones_b[:, :], mask[:, t2, :],
                           start=(t2 == 0), stop=(t2 == tt))
                for t2 in range(nt):
                    last = mm(bank[6][:, NE * nt:NE * nt + NE], ones_b[:, :], mask[:, t2, :],
                              start=(t2 == 0), stop=(t2 == nt - 1))
                last.then_inc(rank_mm, 1)

            def experts(l):
                def turn_rows(n):
                    pe.wait_ge(hc_in[l], 16 * n + 16)
                    for k in range(KD):
                        last = turn(bank[5 + k // 4][:, P * (k % 4):P * (k % 4) + P], hc[:, P * k:P * k + P], ident)
                    last.then_inc(hc_turned[l], 1)

                def chunk(a, turns, g):
                    w = [ring[:, 3 * a + s, :].rearrange("p (k n) -> p k n", k=KD) for s in range(2)]
                    wd = ring[:, 3 * a + 2, :].rearrange("p (k n) -> p k n", k=KF)
                    pe.wait_ge(hc_ready[l], g + 1)
                    for half in range(2):
                        for s in range(2):
                            if half == 0:
                                pe.wait_ge(ew_in[l][3 * a + s], 16 * turns)
                            for k in range(KD):
                                last = mm(bank[1 + half][:, 256 * s:256 * s + 256], hc_t[:, k, :],
                                          w[s][:, k, 256 * half:256 * half + 256], start=(k == 0), stop=(k == KD - 1))
                        last.then_inc(gu_mm[l], 1)
                    turn_rows(g + 1)
                    for half in range(2):
                        pe.wait_ge(he_ready[l], 2 * g + 1 + half)
                        for q in range(2):
                            last = turn(bank[(3, 1)[half]][:, P * q:P * q + P],
                                        he[:, 256 * half + P * q:256 * half + P * q + P], ident)
                        last.then_inc(he_turned[l], 1)
                    pe.wait_ge(ew_in[l][3 * a + 2], 16 * turns)
                    pe.wait_ge(rows_ready[l], g + 1)
                    for k in range(KF):
                        if k % 2 == 0:
                            pe.wait_ge(het_ready[l], 2 * g + 1 + k // 2)
                        for n in range(2):
                            last = mm(bank[(4, 7)[n]][:, :], he_t[:, k, :], wd[:, k, 512 * n:512 * n + 512],
                                      start=(k == 0), stop=(k == KF - 1))
                    last.then_inc(down_mm[l], 1)

                def expert(e, a, turns):
                    g0 = pe.value_load(first[0:1, bass.ds(e, 1)], min_val=0, max_val=MAX_CHUNKS[l])
                    g1 = pe.value_load(first[0:1, bass.ds(e + 1, 1)], min_val=0, max_val=MAX_CHUNKS[l])
                    with pe.Fori(g0, g1) as g:
                        chunk(a, turns, g)
                    mm(bank[0][:, 0:1], ones[:, :], ones[:, 0:1], start=True, stop=True).then_inc(set_free[l][a], 1)

                pe.wait_ge(route_ready, l + 1)
                turn_rows(0)
                with pe.Fori(0, 5) as i:
                    for a in range(3):
                        expert(3 * i + a, a, i + 1)
                expert(15, 0, 6)

            def combine(l):
                nt = TOK_TILES[l]
                tb = sum(TOK_TILES[:l])
                for tt in range(nt):
                    pe.wait_ge(y_summed, tb + tt + 1)
                    if tt >= 2:
                        pe.wait_ge(xc_ready, tb + tt - 1)
                    for k in range(KD):
                        last = turn(bank[1 + 2 * (tt % 2) + k // 4][:, P * (k % 4):P * (k % 4) + P],
                                    tokm[:, tt, P * k:P * k + P], ident)
                    last.then_inc(c_turned, 1)

            pe.wait_ge(cst_in, 16)
            pe.wait_ge(vec_in, 16 * 15)
            turn(bank[0][:, 0:96], vec_a, ident[0:96, 0:96])
            turn(bank[0][:, 96:V_END], vec_b, ident[0:V_END - 96, 0:V_END - 96]).then_inc(vec_turned, 1)
            pe.wait_ge(x_in, 32)
            for k in range(KD):
                if k >= 6:
                    pe.wait_ge((xt_act, xt_dve)[k % 2], 1)
                for tt in range(4):
                    last = turn(bank[1 + k % 6][:, P * tt:P * tt + P], tokm[:, tt, P * k:P * k + P], ident)
                last.then_inc(x_turned, 1)
            pe.wait_ge(ones_set, 1)
            pe.wait_ge(silu_ready, 1)
            pe.wait_ge(bank7_set, 1)
            for l in range(DEPTH):
                norm_sums(2 * l, 512)
                if l == 0:
                    for u in range(4):
                        ada_unit(u)
                        ada_turn(u)
                qkv(l)
                attention(l)
                project_out(l)
                norm_sums(2 * l + 1, P * TOK_TILES[l])
                if l == 0:
                    pe.wait_ge(small_in, 32)
                route(l)
                experts(l)
                combine(l)
            pe.wait_ge(xc_ready, sum(TOK_TILES))
            for tt in range(2):
                for k in range(KD):
                    last = turn(bank[(5, 6, 0, 7)[2 * tt + k // 4]][:, P * (k % 4):P * (k % 4) + P],
                                x_t[:, k, P * tt:P * tt + P], ident)
                last.then_inc(o_turned, 1)

        @block.scalar
        def _(act):
            do = nc.scalar.activation

            def norm_squares(n, width, arrived):
                for k in range(KD):
                    arrived(k)
                    if k >= 2:
                        act.wait_ge(sq_used, KD * n + k - 1)
                    do(sq[k % 2][:, 0:width], x_t[:, k, 0:width], ACT.Square).then_inc(sq_ready, 1)
                act.wait_ge(sq_used, KD * (n + 1))
                do(rstd[:, 0:width], bank[0][:, 0:width], ACT.Sqrt, bias=eps[:, 0:1]).then_inc(norm_root, 1)

            def norm_shift(n, width):
                l, w = divmod(n, 2)
                for k in range(KD):
                    act.wait_ge(hs_ready, KD * n + k + 1)
                    for src in range(width // 256):
                        m = l * NMOD + 3 * KD * w + k
                        cols = slice(256 * src, 256 * src + 256)
                        last = do(h_t[:, k, cols], h_t[:, k, cols], ACT.Identity, bias=mods[:, m, src:src + 1])
                    last.then_inc(h_ready, 1)

            def qkv(l):
                widths = [512, 512] + [P * TOK_TILES[l]] * 8

                def root(i):
                    act.wait_ge(qk_stats, 10 * l + i + 1)
                    if 10 * l + i > 0:
                        act.wait_ge(qk_done, 10 * l + i)
                    do(rstd[:, 0:widths[i]], bank[3][:, 0:widths[i]], ACT.Sqrt, bias=eps[:, 1:2]).then_inc(qk_root, 1)

                for i in range(10):
                    n = widths[i]
                    act.wait_ge(qk_mm, 10 * l + i + 1)
                    if i >= 2:
                        act.wait_ge(qk_stats, 10 * l + i - 1)
                    do(sq[i % 2][:, 0:n], bank[1 + i % 2][:, 0:n], ACT.Square)
                    kind = (1, 3)[i] if i < 2 else 2 * ((i - 2) // 4)
                    col = V_QN + DEPTH * kind + l
                    do(qk_t[:, i, 0:n], bank[1 + i % 2][:, 0:n], ACT.Identity,
                       scale=vec[:, col:col + 1]).then_inc(qk_evac, 1)
                    if i >= 1:
                        root(i - 1)
                root(9)
                for q in range(2):
                    act.wait_ge(v_mm, 2 * l + q + 1)
                    do(v_tok[:, 2 * q:2 * q + 2, :].rearrange("p t n -> p (t n)"), bank[5 + q][:, :],
                       ACT.Identity).then_inc(v_ready, 1)

            def ada_parts(u):
                act.wait_ge(ada_used, u + 1)
                if u > 0:
                    act.wait_ge(ada_turned, u)
                do(parts, bank[7][:, :], ACT.Identity).then_inc(parts_ready, 1)

            def attention(l):
                ub = sum(UNITS[:l])
                for n, (tt, T, kv, r) in enumerate(units(l)):
                    kn = keys(tt)[1]
                    head = l * 8 + 4 * kv + r
                    act.wait_ge(max_ready, ub + n + 1)
                    if n >= 4:
                        act.wait_ge(p_turned, ub + n - 3)
                    if T:
                        do(esink[:, n:n + 1], sink[:, head:head + 1], ACT.Exp, bias=negmax[:, n:n + 1])
                    do(probs[:, n % 4, 0:kn], bank[n % 2][:, 0:kn], ACT.Exp, bias=negmax[:, n:n + 1], scale=SCALE,
                       accum_out=lsum[:, n:n + 1]).then_inc(exp_done, 1)
                    if l == 0 and n % 3 == 1 and n // 3 < 20:
                        ada_parts(4 + n // 3)

            def route(l):
                nt = TOK_TILES[l]
                act.wait_ge(lg_mm, l + 1)
                do(work[:, 512:512 + NE * nt], bank[1][:, 0:NE * nt], ACT.Sigmoid).then_inc(sig_ready, 1)
                for q in range(2 * nt):
                    act.wait_ge(h_turned, 2 * sum(TOK_TILES[:l]) + q + 1)
                    do(tokm[:, q // 2, 512 * (q % 2):512 * (q % 2) + 512], bank[2 + q % 4][:, :],
                       ACT.Identity).then_inc(tok_ready, 1)

            def experts(l):
                def chunk_turned(n):
                    act.wait_ge(hc_turned[l], n + 1)
                    do(hc_t[:, 0:4, :].rearrange("p k t -> p (k t)"), bank[5][:, :], ACT.Identity)
                    do(hc_t[:, 4:8, :].rearrange("p k t -> p (k t)"), bank[6][:, :],
                       ACT.Identity).then_inc(hc_ready[l], 1)

                act.wait_ge(route_ready, l + 1)
                total = act.value_load(first[0:1, NE:NE + 1], min_val=1, max_val=MAX_CHUNKS[l])
                chunk_turned(0)
                with act.Fori(0, total) as g:
                    for half in range(2):
                        act.wait_ge(gu_mm[l], 2 * g + 1 + half)
                        do(act_g[:, 256 * half:256 * half + 256], bank[1 + half][:, 0:256],
                           ACT.Silu).then_inc(silu_done[l], 1)
                    chunk_turned(g + 1)
                    act.wait_ge(down_mm[l], g + 1)
                    act.wait_ge(rows_stored[l], 16 * g + 16)
                    do(yrow[:, 0:512], bank[4][:, :], ACT.Identity)
                    do(yrow[:, 512:D], bank[7][:, :], ACT.Identity).then_inc(rows_ready[l], 1)

            def combine(l):
                for tt in range(TOK_TILES[l]):
                    act.wait_ge(yg_in[l][tt], 32)
                    do(ych[0][:, tt, :], ych[0][:, tt, :], ACT.Identity,
                       scale=wgt[:, tt:tt + 1]).then_inc(y_scaled, 1)

            act.dma_start(vec_a, ada_b.rearrange("l (m p) -> (l m) p", p=P)).then_inc(vec_in, 16)

            def vec_rows(row, n, cols, src):
                r = row - 96
                act.dma_start(h_t[r:r + n, 0, P + cols[0]:P + cols[1]], src).then_inc(vec_in, 16)

            vec_rows(V_AG, DEPTH * KD, (0, P), attn_norm_g.rearrange("l (k p) -> (l k) p", p=P))
            vec_rows(V_FG, DEPTH * KD, (0, P), ffn_norm_g.rearrange("l (k p) -> (l k) p", p=P))
            vec_rows(V_C, KD, (0, P), c.rearrange("b (k p) -> (b k) p", p=P))
            vec_rows(V_CC, KD, (0, P), c_ctx.rearrange("(k p) -> k p", p=P))
            for i, g in enumerate((qn_global, kn_global, qn_local, kn_local)):
                for half in range(2):
                    vec_rows(V_QN + DEPTH * i, DEPTH, (HD * half, HD * half + HD), g)
            act.dma_start(sink[:, :], sink_logit.rearrange("l h -> (l h)").partition_broadcast(P)
                          ).then_inc(vec_in, 16)
            act.dma_start(upper_f, table[:, C_UP:C_ALL]).then_inc(vec_in, 16)
            act.dma_start(rb[:, :], router_b.partition_broadcast(P)).then_inc(small_in, 16)
            act.dma_start(rw[:, :, :], router_w.rearrange("(k p) e -> p k e", p=P)).then_inc(small_in, 16)

            act.wait_ge(vec_ready, 1)
            do(scv[:, :, 0], vec[:, V_C:V_C + KD], ACT.Silu)
            do(scv[:, :, 1], vec[:, V_CC:V_CC + KD], ACT.Silu).then_inc(silu_ready, 1)
            for k in range(0, KD, 2):
                act.wait_ge(x_turned, k + 1)
                do(x_t[:, k, :], bank[1 + k % 6][:, :], ACT.Identity).then_inc(xt_act, 1)
            for l in range(DEPTH):
                if l == 0:
                    def arrived(k):
                        act.wait_ge((xt_act, xt_dve)[k % 2], k // 2 + 1)
                else:
                    def arrived(k):
                        act.wait_ge(xc_ready, TOK_TILES[0])
                norm_squares(2 * l, 512, arrived)
                if l == 0:
                    for u in range(4):
                        ada_parts(u)
                norm_shift(2 * l, 512)
                qkv(l)
                attention(l)
                norm_squares(2 * l + 1, P * TOK_TILES[l], lambda k: act.wait_ge(xw_ready, KD * l + k + 1))
                norm_shift(2 * l + 1, P * TOK_TILES[l])
                route(l)
                experts(l)
                combine(l)
            for tt in range(2):
                act.wait_ge(o_turned, tt + 1)
                do(out_tok[:, tt, 0:512], bank[(5, 0)[tt]][:, :], ACT.Identity).then_inc(o_act, 1)

        @block.gpsimd
        def _(pool):
            for l in range(DEPTH):
                nt = TOK_TILES[l]
                pool.wait_ge(qk_done, 10 * (l + 1))
                for T in range(2):
                    for a in range(2):
                        pool.dma_start(sq[T][HD * a:HD * a + HD, :], qk_t[HD * (1 - a):HD * (2 - a), T, :]
                                       ).then_inc(swapped, 16)
                pool.wait_ge(rows_ready[l], 1)
                pool.dma_start(h_rows[ROWS:ROWS + CHUNK, :], yrow).then_inc(rows_stored[l], 16)
                pool.wait_ge(tok_ready, 2 * sum(TOK_TILES[:l + 1]))
                pool.wait_ge(route_ready, l + 1)
                for tt in range(nt):
                    for s in range(2):
                        pool.indirect_dma_start(h_rows[0:2 * nt * P, :],
                                                bass.IndirectOffsetOnAxis(posidx[:, nt * s + tt:nt * s + tt + 1], 0),
                                                tokm[:, tt, :], None).then_inc(scattered, 16)
                pool.wait_ge(scattered, 32 * sum(TOK_TILES[:l + 1]))
                pool.wait_ge(rows_stored[l], 16)

                def row_of(n):
                    return pool.value_load(chunk_row[0:1, bass.ds(n, 1)], min_val=0, max_val=ROWS)

                def load_rows(n):
                    pool.dma_start(hc, h_rows[bass.ds(row_of(n), CHUNK), :]).then_inc(hc_in[l], 16)

                load_rows(0)
                total = pool.value_load(first[0:1, NE:NE + 1], min_val=1, max_val=MAX_CHUNKS[l])
                pool.wait_ge(hc_turned[l], 1)
                load_rows(1)
                with pool.Fori(0, total) as g:
                    pool.wait_ge(hc_turned[l], g + 2)
                    load_rows(g + 2)
                    pool.wait_ge(rows_ready[l], g + 2)
                    pool.dma_start(y_rows[bass.ds(row_of(g), CHUNK), :], yrow).then_inc(rows_stored[l], 16)
                pool.wait_ge(rows_stored[l], total * 16 + 16)
                pool.wait_ge(hc_in[l], total * 16 + 32)
                pool.sem_inc(rows_all, 1)
                pool.wait_ge(rows_all, l + 1)
                for tt in range(nt):
                    for s in range(2):
                        pool.indirect_dma_start(ych[s][:, tt, :], None, y_rows[0:2 * nt * P, :],
                                                bass.IndirectOffsetOnAxis(posidx[:, nt * s + tt:nt * s + tt + 1], 0)
                                                ).then_inc(yg_in[l][tt], 16)

        @block.vector
        def _(dve):
            v = nc.vector
            chain = [0]

            def link(ins):
                chain[0] += 1
                ins.then_inc(dve_step, 1)
                dve.wait_ge(dve_step, chain[0])

            def gains(l):
                for w in range(2):
                    m = l * NMOD + (3 * w + 1) * KD
                    g0 = (V_AG, V_FG)[w] + l * KD
                    link(v.tensor_scalar(gain[:, l, w], mods[:, m:m + KD, :], 1.0, D ** 0.5, ALU.add, ALU.mult))
                    gv = vec[:, g0:g0 + KD].unsqueeze(2).to_broadcast([P, KD, 2])
                    link(v.tensor_tensor(gain[:, l, w], gain[:, l, w], gv, ALU.mult))

            def ada_sum(u):
                dve.wait_ge(ada_turned, u + 1)
                ps = bank[2][:, :].rearrange("p (m q x) -> p m x q", m=4, q=4)[:, :, 0:2, :]
                v.tensor_reduce(mods[:, 4 * u:4 * u + 4, :], ps, AX.X, ALU.add).then_inc(ada_summed, 1)

            def add_bias(m0, m1):
                dve.wait_ge(ada_summed, m1 // 4)
                bias = vec[:, V_ADAB + m0:V_ADAB + m1].unsqueeze(2).to_broadcast([P, m1 - m0, 2])
                link(v.tensor_tensor(mods[:, m0:m1, :], mods[:, m0:m1, :], bias, ALU.add))

            def norm_scale(n, width):
                l, w = divmod(n, 2)
                dve.wait_ge(norm_root, n + 1)
                link(v.reciprocal(rstd[:, 0:width], rstd[:, 0:width]))
                for k in range(KD):
                    for src in range(width // 256):
                        cols = slice(256 * src, 256 * src + 256)
                        last = v.scalar_tensor_tensor(out=h_t[:, k, cols], in0=x_t[:, k, cols],
                                                      scalar=gain[:, l, w, k, src:src + 1], in1=rstd[:, cols],
                                                      op0=ALU.mult, op1=ALU.mult)
                    last.then_inc(hs_ready, 1)

            def qk_norms(l):
                widths = [512, 512] + [P * TOK_TILES[l]] * 8
                for i in range(10):
                    n = widths[i]
                    dve.wait_ge(qk_root, 10 * l + i + 1)
                    v.reciprocal(rstd[:, 0:n], rstd[:, 0:n])
                    v.tensor_tensor(rope_a, qk_t[:, i, 0:SEQ], cos, ALU.mult)
                    link(v.tensor_tensor(rope_b, bank[4][:, 0:SEQ], sin, ALU.mult))
                    link(v.tensor_tensor(qk_t[:, i, 0:SEQ], rope_a, rope_b, ALU.add))
                    v.scalar_tensor_tensor(out=qk_t[:, i, 0:n], in0=qk_t[:, i, 0:n], scalar=float(HD ** 0.5),
                                           in1=rstd[:, 0:n], op0=ALU.mult, op1=ALU.mult).then_inc(qk_done, 1)
                    dve.wait_ge(qk_done, 10 * l + i + 1)

            def attention(l):
                ub, gb = sum(UNITS[:l]), sum(UNITS[:l]) // 4
                us = units(l)
                nu = UNITS[l]
                dve.wait_ge(v_mm, 2 * (l + 1))
                link(v.memset(esink[:, 0:nu], 0.0))
                dve.sem_inc(esink_set, 1)

                def maxima(n):
                    tt, T, kv, r = us[n]
                    head = l * 8 + 4 * kv + r
                    dve.wait_ge(sc_done, ub + n + 1)
                    link(v.tensor_reduce(smx[:, n:n + 1], bank[n % 2][:, 0:keys(tt)[1]], AX.X, ALU.max))
                    if T:
                        ins = v.tensor_scalar(negmax[:, n:n + 1], smx[:, n:n + 1], -SCALE, nsink[:, head:head + 1],
                                              ALU.mult, ALU.min)
                    else:
                        ins = v.tensor_scalar(negmax[:, n:n + 1], smx[:, n:n + 1], -SCALE, None, ALU.mult)
                    ins.then_inc(max_ready, 1)

                def scale_probs(n):
                    kn = keys(us[n][0])[1]
                    dve.wait_ge(exp_done, ub + n + 1)
                    if us[n][1]:
                        link(v.tensor_tensor(lsum[:, n:n + 1], lsum[:, n:n + 1], esink[:, n:n + 1], ALU.add))
                    link(v.reciprocal(lrec[:, n:n + 1], lsum[:, n:n + 1]))
                    v.tensor_scalar(probs[:, n % 4, 0:kn], probs[:, n % 4, 0:kn], lrec[:, n:n + 1], None,
                                    ALU.mult).then_inc(p_scaled, 1)

                def probs_out(n):
                    nk = keys(us[n][0])[1] // P
                    g, r = divmod(n, 4)
                    dve.wait_ge(p_turned, ub + n + 1)
                    if r == 0 and g >= 1:
                        dve.wait_ge(pv_done, gb + g)
                    col = 256 * (r % 2) + P * (r // 2)
                    v.tensor_copy(probs_t[:, 0:nk, col:col + P],
                                  bank[4 + n % 2][:, 0:P * nk].rearrange("p (k q) -> p k q", k=nk)).then_inc(pt_ready, 1)

                def y_out(g):
                    tt, T, kv, _ = us[4 * g]
                    dve.wait_ge(pv_done, gb + g + 1)
                    k = 4 * T + 2 * kv
                    v.tensor_copy(y_t[:, k:k + 2, P * tt:P * tt + P],
                                  bank[(3, 6)[g % 2]][:, 0:256].rearrange("p (i q) -> p i q", i=2)).then_inc(y_evac, 1)

                for n in range(nu + 4):
                    if n < nu:
                        maxima(n)
                    if 1 <= n < nu + 1:
                        scale_probs(n - 1)
                    if n >= 7 and n % 4 == 3:
                        y_out(n // 4 - 1)
                    if 2 <= n < nu + 2:
                        probs_out(n - 2)
                    if l == 0 and n % 3 == 2 and n // 3 < 20:
                        ada_sum(4 + n // 3)

            def add_attention(l):
                for m in range(KD):
                    dve.wait_ge(wo_mm, KD * l + m + 1)
                    for src in range(TOK_TILES[l] // 2):
                        cols = slice(256 * src, 256 * src + 256)
                        mod = l * NMOD + 2 * KD + m
                        last = v.scalar_tensor_tensor(out=x_t[:, m, cols], in0=bank[4 + m % 2][:, cols],
                                                      scalar=mods[:, mod, src:src + 1], in1=x_t[:, m, cols],
                                                      op0=ALU.mult, op1=ALU.add)
                    last.then_inc(xw_ready, 1)

            def route(l):
                nt = TOK_TILES[l]
                n16 = NE * nt

                def tmp(i):
                    return work[:, 64 * i:64 * i + n16]

                def te(a):
                    return a.rearrange("p (t e) -> p t e", t=nt)

                eq, sel, oh1, oh2, cand, rank = (tmp(i) for i in (1, 2, 3, 4, 5, 6))
                mask = mask_b[:, 0:n16]
                sc = work[:, 512:512 + n16]
                hi = work[:, 576:576 + 8 * nt]
                lo = work[:, 608:608 + 8 * nt]
                g4 = [work[:, 640 + 16 * i:640 + 16 * i + 4 * nt] for i in range(5)]
                t1 = [work[:, 720 + 4 * i:720 + 4 * i + nt] for i in range(4)]
                tot = work[:, 768:768 + NE]
                nch = work[:, 784:784 + NE]
                firstf = work[:, 800:800 + NE + 1]
                cmp = work[:, 832:832 + NE * (MAXCH - 1)]
                tri = work[:, 960:960 + NE * (NE + 1)]
                base = work[:, 880:880 + NE + 1]
                rowf = work[:, 900:900 + GT]
                owns = [hflat[:, 1024 + 512 * i:1024 + 512 * i + GT * NE].rearrange("p (g e) -> p g e", e=NE)
                        for i in range(2)]

                def per_tile(a, n):
                    return a.unsqueeze(2).to_broadcast([P, nt, n])

                def best(values, keys_, weights, n, hot, e4, c4):
                    link(v.tensor_reduce(t1[0], values, AX.X, ALU.max))
                    link(v.tensor_tensor(e4, values, per_tile(t1[0], n), ALU.is_equal))
                    link(v.tensor_tensor(c4, e4, weights.unsqueeze(1).to_broadcast([P, nt, n]), ALU.mult))
                    link(v.tensor_reduce(t1[0], c4, AX.X, ALU.max))
                    link(v.tensor_tensor(hot, c4, per_tile(t1[0], n), ALU.is_equal))

                dve.wait_ge(sig_ready, l + 1)
                if l == 0:
                    dve.wait_ge(small_in, 32)
                link(v.tensor_tensor(te(sel), te(sc), rb[:, :].unsqueeze(1).to_broadcast([P, nt, NE]), ALU.add))
                pair = sel.rearrange("p (g j i) -> p g j i", j=2, i=2)
                hi3 = hi.rearrange("p (g j) -> p g j", j=2)
                lo3 = lo.rearrange("p (g j) -> p g j", j=2)
                v.tensor_tensor(hi3, pair[:, :, :, 0], pair[:, :, :, 1], ALU.max)
                link(v.tensor_tensor(lo3, pair[:, :, :, 0], pair[:, :, :, 1], ALU.min))
                v.tensor_tensor(g4[0], hi3[:, :, 0], hi3[:, :, 1], ALU.max)
                v.tensor_tensor(g4[1], hi3[:, :, 0], hi3[:, :, 1], ALU.min)
                link(v.tensor_tensor(g4[2], lo3[:, :, 0], lo3[:, :, 1], ALU.max))
                link(v.tensor_tensor(g4[1], g4[1], g4[2], ALU.max))
                link(v.tensor_tensor(g4[0], g4[0], g4[1], ALU.add))
                tg = [a.rearrange("p (t g) -> p t g", t=nt) for a in g4]
                best(tg[0], None, cst[:, C_W4:C_W4 + NG], NG, tg[3], tg[1], tg[2])
                link(v.tensor_scalar(g4[4], g4[3], 1.0, BIG, ALU.subtract, ALU.mult))
                link(v.tensor_tensor(sel.rearrange("p (g i) -> p g i", i=EPG), sel.rearrange("p (g i) -> p g i", i=EPG),
                                     g4[4].unsqueeze(2).to_broadcast([P, NG * nt, EPG]), ALU.add))
                best(te(sel), None, cst[:, C_W16:C_W16 + NE], NE, te(oh1), te(eq), te(cand))
                link(v.scalar_tensor_tensor(out=sel, in0=oh1, scalar=-3e38, in1=sel, op0=ALU.mult, op1=ALU.add))
                best(te(sel), None, cst[:, C_W16:C_W16 + NE], NE, te(oh2), te(eq), te(cand))
                v.tensor_tensor(mask, oh1, oh2, ALU.add).then_inc(mask_ready, 1)
                for s, oh in enumerate((oh1, oh2)):
                    link(v.tensor_tensor(eq, oh, sc, ALU.mult))
                    link(v.tensor_reduce(t1[1 + s], te(eq), AX.X, ALU.add))
                link(v.tensor_tensor(t1[3], t1[1], t1[2], ALU.add))
                link(v.reciprocal(t1[3], t1[3]))
                v.tensor_tensor(wgt[:, 0:nt], t1[1], t1[3], ALU.mult)
                v.tensor_tensor(wgt[:, nt:2 * nt], t1[2], t1[3], ALU.mult)
                dve.wait_ge(rank_mm, l + 1)
                v.tensor_copy(rank, bank[6][:, 0:n16])
                link(v.tensor_copy(tot, bank[6][:, n16:n16 + NE]))
                fe = cst[:, C_TRI:C_THR].rearrange("p (f e) -> p f e", e=NE)
                tri3 = tri.rearrange("p (f e) -> p f e", e=NE)
                link(v.tensor_tensor(tri3, tot.unsqueeze(1).to_broadcast([P, NE + 1, NE]), fe, ALU.mult))
                link(v.tensor_reduce(base, tri3, AX.X, ALU.add))
                link(v.tensor_tensor(te(rank), te(rank), base[:, 0:NE].unsqueeze(1).to_broadcast([P, nt, NE]), ALU.add))
                for s, oh in enumerate((oh1, oh2)):
                    link(v.tensor_tensor(eq, oh, rank, ALU.mult))
                    link(v.tensor_reduce(pos[:, nt * s:nt * s + nt], te(eq), AX.X, ALU.add))
                v.tensor_copy(posidx[:, 0:2 * nt], pos[:, 0:2 * nt])
                link(v.tensor_tensor(cmp.rearrange("p (e j) -> p e j", e=NE), tot.unsqueeze(2).to_broadcast([P, NE, MAXCH - 1]),
                                     cst[:, C_THR:C_W16].unsqueeze(1).to_broadcast([P, NE, MAXCH - 1]), ALU.is_gt))
                link(v.tensor_reduce(nch, cmp.rearrange("p (e j) -> p e j", e=NE), AX.X, ALU.add))
                link(v.tensor_scalar(nch, nch, 1.0, None, ALU.add))
                link(v.tensor_tensor(tri3, nch.unsqueeze(1).to_broadcast([P, NE + 1, NE]), fe, ALU.mult))
                link(v.tensor_reduce(firstf, tri3, AX.X, ALU.add))
                v.tensor_copy(first[:, :], firstf)
                link(v.scalar_tensor_tensor(out=base[:, 0:NE], in0=firstf[:, 0:NE], scalar=-float(CHUNK),
                                            in1=base[:, 0:NE], op0=ALU.mult, op1=ALU.add))
                gs = cst[:, C_G:C_G + GT].unsqueeze(2).to_broadcast([P, GT, NE])
                v.tensor_tensor(owns[0], gs, firstf[:, 0:NE].unsqueeze(1).to_broadcast([P, GT, NE]), ALU.is_ge)
                link(v.tensor_tensor(owns[1], gs, firstf[:, 1:NE + 1].unsqueeze(1).to_broadcast([P, GT, NE]), ALU.is_ge))
                link(v.tensor_tensor(owns[0], owns[0], owns[1], ALU.subtract))
                link(v.scalar_tensor_tensor(out=owns[1], in0=gs, scalar=float(CHUNK),
                                            in1=base[:, 0:NE].unsqueeze(1).to_broadcast([P, GT, NE]),
                                            op0=ALU.mult, op1=ALU.add))
                link(v.tensor_tensor(owns[0], owns[0], owns[1], ALU.mult))
                link(v.tensor_reduce(rowf, owns[0], AX.X, ALU.add))
                link(v.tensor_copy(chunk_row[:, :], rowf))
                dve.sem_inc(route_ready, 1)
                dve.wait_ge(sq_used, 8 * (2 * l + 2))
                v.memset(yrow, 0.0).then_inc(rows_ready[l], 1)

            def experts(l):
                total = dve.value_load(first[0:1, NE:NE + 1], min_val=1, max_val=MAX_CHUNKS[l])
                with dve.Fori(0, total) as g:
                    for half in range(2):
                        cols = slice(256 * half, 256 * half + 256)
                        dve.wait_ge(silu_done[l], 2 * g + 1 + half)
                        v.tensor_tensor(he[:, cols], bank[1 + half][:, 256:512], act_g[:, cols],
                                        ALU.mult).then_inc(he_ready[l], 1)
                    for half in range(2):
                        dve.wait_ge(he_turned[l], 2 * g + 1 + half)
                        v.tensor_copy(he_t[:, 2 * half:2 * half + 2, :].rearrange("p k t -> p (k t)"),
                                      bank[(3, 1)[half]][:, 0:256]).then_inc(het_ready[l], 1)

            def combine(l):
                nt = TOK_TILES[l]
                tb = sum(TOK_TILES[:l])

                def add_rows(tt):
                    dve.wait_ge(c_turned, tb + tt + 1)
                    for k in range(KD):
                        mod = l * NMOD + 5 * KD + k
                        ps = bank[1 + 2 * (tt % 2) + k // 4][:, P * (k % 4):P * (k % 4) + P]
                        xs = x_t[:, k, P * tt:P * tt + P]
                        last = v.scalar_tensor_tensor(out=xs, in0=ps, scalar=mods[:, mod, tt // 2:tt // 2 + 1],
                                                      in1=xs, op0=ALU.mult, op1=ALU.add)
                    last.then_inc(xc_ready, 1)

                for tt in range(nt):
                    dve.wait_ge(y_scaled, tb + tt + 1)
                    v.scalar_tensor_tensor(out=ych[0][:, tt, :], in0=ych[1][:, tt, :],
                                           scalar=wgt[:, nt + tt:nt + tt + 1], in1=ych[0][:, tt, :],
                                           op0=ALU.mult, op1=ALU.add).then_inc(y_summed, 1)
                    if tt >= 1:
                        add_rows(tt - 1)
                add_rows(nt - 1)

            v.memset(eps[:, 0:1], D * EPS)
            v.memset(eps[:, 1:2], HD * EPS)
            v.memset(ones[:, :], 1.0).then_inc(ones_set, 1)
            v.memset(bank[7][:, :], 0.0).then_inc(bank7_set, 1)
            dve.wait_ge(vec_turned, 1)
            v.tensor_copy(vec[:, :], bank[0][:, 0:V_END]).then_inc(vec_ready, 1)
            dve.wait_ge(vec_in, 16 * 15)
            v.memset(ones_b[:, :], 1.0)
            link(v.tensor_copy(upper_b[:, :], upper_f))
            link(v.tensor_scalar(nsink[:, :], sink[:, :], -1.0, None, ALU.mult))
            for k in range(1, KD, 2):
                dve.wait_ge(x_turned, k + 1)
                v.tensor_copy(x_t[:, k, :], bank[1 + k % 6][:, :]).then_inc(xt_dve, 1)
            for u in range(4):
                ada_sum(u)
            add_bias(0, 2 * KD)
            link(v.tensor_scalar(gain[:, 0, 0], mods[:, KD:2 * KD, :], 1.0, D ** 0.5, ALU.add, ALU.mult))
            link(v.tensor_tensor(gain[:, 0, 0], gain[:, 0, 0],
                                 vec[:, V_AG:V_AG + KD].unsqueeze(2).to_broadcast([P, KD, 2]), ALU.mult))
            dve.sem_inc(mods_ready, 1)
            for l in range(DEPTH):
                norm_scale(2 * l, 512)
                qk_norms(l)
                attention(l)
                if l == 0:
                    add_bias(2 * KD, DEPTH * NMOD)
                    gains(0)
                    gains(1)
                    dve.sem_inc(mods_ready, 1)
                add_attention(l)
                norm_scale(2 * l + 1, P * TOK_TILES[l])
                route(l)
                experts(l)
                combine(l)
            for tt in range(2):
                dve.wait_ge(o_turned, tt + 1)
                v.tensor_copy(out_tok[:, tt, 512:D], bank[(6, 7)[tt]][:, :]).then_inc(o_dve, 1)


_INS = ['x', 'c', 'ctx', 'c_ctx', 'ada_w', 'ada_b', 'attn_norm_g', 'ffn_norm_g', 'w_in', 'qn_global', 'kn_global',
        'qn_local', 'kn_local', 'sink_logit', 'w_out', 'router_w', 'router_b', 'w_gate', 'w_up', 'w_down']


def kernel(**inputs):
    import numpy as _np
    import concourse.bacc as _bacc
    from concourse import mybir as _mybir
    from concourse.bass_utils import run_bass_kernel_spmd as _run

    nc = _bacc.Bacc("TRN2", target_bir_lowering=False, num_devices=1)
    arrays, args = {}, []
    for name in _INS:
        a = _np.ascontiguousarray(inputs[name])
        arrays[f"in_{name}_dram"] = a
        args.append(nc.dram_tensor(f"in_{name}_dram", a.shape, _mybir.dt.from_np(a.dtype), kind="ExternalInput").ap())
    a = constants()
    arrays["in_table_dram"] = a
    args.append(nc.dram_tensor("in_table_dram", a.shape, _mybir.dt.from_np(a.dtype), kind="ExternalInput").ap())
    out = nc.dram_tensor("out_dram", (1, SEQ, D), F32, kind="ExternalOutput").ap()
    backbone(nc, *args, out)
    r = _run(nc, [arrays], core_ids=[0])
    return r.results[0]["out_dram"]
```

```python
from contextlib import ExitStack

import concourse.bass as bass
from concourse import mybir

F32 = mybir.dt.float32
I32 = mybir.dt.int32
BF16 = mybir.dt.bfloat16
U32 = mybir.dt.uint32
ALU = mybir.AluOpType
ACT = mybir.ActivationFunctionType
AX = mybir.AxisListType

P = 128
D = 1024
KD = D // P
SEQ = 256
CTX = 256
DEPTH = 2
HD = 64
NE = 16
NG = 4
EPG = NE // NG
FE = 512
KF = FE // P
NMOD = 6 * KD
EPS = 1e-6
SCALE = HD ** -0.5
NEG = -1e30
BIG = 1e30

TOK_TILES = [(SEQ + CTX) // P, SEQ // P]
UNITS = [16 * t for t in TOK_TILES]
SHORT = P // 2
CHUNK = [P, SHORT]
MAXCH = TOK_TILES[0] * P // CHUNK[0]
MAX_CHUNKS = [NE + 2 * t * P // n for t, n in zip(TOK_TILES, CHUNK)]
GT = max(MAX_CHUNKS) + 2
ROWS = 2 * (SEQ + CTX)

C_ID, C_BLK, C_SWP = 0, P, 2 * P
C_COS = 3 * P
C_SIN = C_COS + SEQ
C_M0 = C_SIN + SEQ
C_M1 = C_M0 + P
C_G = C_M1 + P
C_TRI = C_G + GT
C_THR = C_TRI + (NE + 1) * NE
C_W16 = C_THR + DEPTH * (MAXCH - 1)
C_W4 = C_W16 + NE
C_END = C_W4 + NG
C_UP = C_END
C_ALL = C_UP + P

V_ADAB = 0
V_AG = DEPTH * NMOD
V_FG = V_AG + DEPTH * KD
V_C = V_FG + DEPTH * KD
V_CC = V_C + KD
V_QN = V_CC + KD
V_END = V_QN + 4 * DEPTH


def constants():
    import numpy as np
    t = np.zeros((P, C_ALL), np.float32)
    i = np.arange(P)
    t[:, C_ID:C_ID + P] = np.eye(P)
    t[:, C_UP:C_UP + P] = i[:, None] < i[None, :]
    t[:, C_BLK:C_BLK + P] = i[:, None] // HD == i[None, :] // HD
    t[:, C_SWP:C_SWP + P] = (i[:, None] ^ 16) == i[None, :]
    tok = np.arange(SEQ)
    grid = np.stack([tok // 64, tok % 64]).astype(np.float32)
    nf = HD // 4
    inv = np.float32(10000.0) ** (-np.arange(nf, dtype=np.float32) / np.float32(nf))
    d = i % HD
    ang = (grid[d // 32] * inv[d % nf][:, None]).astype(np.float32)
    t[:, C_COS:C_COS + SEQ] = np.cos(ang)
    t[:, C_SIN:C_SIN + SEQ] = np.where((d % 32 < 16)[:, None], -np.sin(ang), np.sin(ang))
    t[:, C_M0:C_M0 + P] = np.where(i[None, :] > i[:, None], NEG, 0.0)
    t[:, C_M1:C_M1 + P] = np.where(i[None, :] < i[:, None], NEG, 0.0)
    t[:, C_G:C_G + GT] = np.arange(GT)
    e = np.arange(NE)
    t[:, C_TRI:C_THR] = (e[None, :] < np.arange(NE + 1)[:, None]).reshape(-1)
    for l in range(DEPTH):
        t[:, C_THR + l * (MAXCH - 1):C_THR + (l + 1) * (MAXCH - 1)] = CHUNK[l] * np.arange(1, MAXCH)
    t[:, C_W16:C_W4] = NE - e
    t[:, C_W4:C_END] = NG - np.arange(NG)
    return t


def backbone(nc, x, c, ctx_in, c_ctx, ada_w, ada_b, attn_norm_g, ffn_norm_g, w_in, qn_global, kn_global,
             qn_local, kn_local, sink_logit, w_out, router_w, router_b, w_gate, w_up, w_down, table, out):
    with ExitStack() as stack:
        def sb(name, shape, dt=F32):
            return stack.enter_context(nc.sbuf_tensor(name, shape, dt))

        def sem(name):
            return stack.enter_context(nc.semaphore(name))

        def per_layer(name):
            return [sem(f"{name}{l}") for l in range(DEPTH)]

        ring = sb("ring", [P, 9, 4096])
        x_t = sb("x_t", [P, KD, 512])
        h_t = sb("h_t", [P, KD, 512])
        tokm = sb("tokm", [P, 4, D])
        cst = sb("cst", [P, C_END])
        ones = sb("ones", [P, P])
        eps = sb("eps", [P, 2])
        rw = sb("rw", [P, KD, NE])
        rb = sb("rb", [P, NE])
        sink = sb("sink", [P, DEPTH * 8])
        nsink = sb("nsink", [P, DEPTH * 8])
        work = sb("work", [P, 1536])
        vec = sb("vec", [P, V_END])
        scv = sb("scv", [P, KD, 2])
        mods = sb("mods", [P, DEPTH * NMOD, 2])
        gain = sb("gain", [P, DEPTH, 2, KD, 2])
        upper_b = sb("upper_b", [P, P], BF16)
        ones_b = sb("ones_b", [P, P], BF16)
        mask_b = sb("mask_b", [P, 64], BF16)
        pos = sb("pos", [P, 8])
        posidx = sb("posidx", [P, 8], U32)
        wgt = sb("wgt", [P, 8])
        first = sb("first", [P, NE + 1], I32)
        short = sb("short", [P, NE], I32)
        chunk_row = sb("chunk_row", [P, GT], I32)

        bank = [stack.enter_context(nc.psum_tensor(f"bank{i}", [P, 512], F32)) for i in range(8)]
        h_rows = nc.dram_tensor("h_rows", [ROWS + P, D], F32, kind="Internal").ap()
        y_rows = nc.dram_tensor("y_rows", [ROWS + P, D], F32, kind="Internal").ap()

        ident = cst[:, C_ID:C_ID + P]
        head_ones = cst[:, C_BLK:C_BLK + P]
        swap = cst[:, C_SWP:C_SWP + P]
        cos = cst[:, C_COS:C_COS + SEQ]
        sin = cst[:, C_SIN:C_SIN + SEQ]
        band = [cst[:, C_M0:C_M0 + P], cst[:, C_M1:C_M1 + P]]
        upper_f = h_t[:, 0, 2 * P:3 * P]

        vec_a = h_t[0:96, 0, 0:P]
        vec_b = h_t[0:V_END - 96, 0, P:2 * P]
        sq = [work[:, 0:512], work[:, 512:1024]]
        rstd = work[:, 1024:1536]
        win = ring[:, 3:6, :].rearrange("p a b -> p (a b)").rearrange("p (k n) -> p k n", k=KD)
        wout = [ring[:, 6, :].rearrange("p (k n) -> p k n", k=4), ring[:, 3, :].rearrange("p (k n) -> p k n", k=4)]
        scratch = ring[:, 7:9, :].rearrange("p a b -> p (a b)")
        qk_t = scratch[:, 0:5120].rearrange("p (i n) -> p i n", i=10)
        v_tok = scratch[:, 5120:6144].rearrange("p (t n) -> p t n", t=4)
        probs = scratch[:, 6144:8192].rearrange("p (b n) -> p b n", b=4)
        rope_a = probs[:, 0, 0:SEQ]
        rope_b = probs[:, 1, 0:SEQ]
        probs_t = h_t[:, 0:4, :]
        parts = h_t[:, 5, :]
        y_t = tokm[:, :, :].rearrange("p t n -> p (t n)").rearrange("p (k n) -> p k n", k=KD)
        smx = h_t[:, 4, 0:64]
        negmax = h_t[:, 4, 64:128]
        lsum = h_t[:, 4, 128:192]
        esink = h_t[:, 4, 192:256]
        lrec = h_t[:, 4, 256:320]
        hflat = h_t[:, :, :].rearrange("p k n -> p (k n)")
        hc = hflat[:, 0:1024]
        hc_t = hflat[:, 1024:2048].rearrange("p (k t) -> p k t", k=KD)
        act_g = hflat[:, 2048:2560]
        he = hflat[:, 2560:3072]
        he_t = hflat[:, 3072:3584].rearrange("p (k t) -> p k t", k=KF)
        yrow = work[:, 0:1024]
        ych = [tokm, hflat.rearrange("p (t n) -> p t n", t=4)]
        tile_sq = [ych[1][:, t, :].rearrange("p (k t) -> p k t", k=KD) for t in range(4)]
        out_tok = ring[:, 0:1, :].rearrange("p a b -> p (a b)")[:, 0:2 * D].rearrange("p (t n) -> p t n", t=2)

        cst_in, vec_in, x_in, small_in = sem("cst_in"), sem("vec_in"), sem("x_in"), sem("small_in")
        ada_in = [sem(f"ada_in{s}") for s in range(4)]
        ada2_in = [sem(f"ada2_in{s}") for s in range(4)]
        win_in = [sem(f"win_in{s}") for s in range(4)]
        wout_in = [sem(f"wout_in{s}") for s in range(2)]
        ew_in = [[sem(f"ew_in{l}_{s}") for s in range(9)] for l in range(DEPTH)]
        set_free = [[sem(f"set_free{l}_{s}") for s in range(3)] for l in range(DEPTH)]
        ones_set = sem("ones_set")
        vec_turned, vec_ready, silu_ready = sem("vec_turned"), sem("vec_ready"), sem("silu_ready")
        x_turned, xt_act, xt_dve = sem("x_turned"), sem("xt_act"), sem("xt_dve")
        ada_used, mods_ready = sem("ada_used"), sem("mods_ready")
        bank7_set, parts_ready, ada_turned, ada_summed = (sem(n) for n in ("bank7_set", "parts_ready", "ada_turned",
                                                                           "ada_summed"))
        sq_ready, sq_used, sq_added = sem("sq_ready"), sem("sq_used"), sem("sq_added")
        tile_squared, sums_done = sem("tile_squared"), sem("sums_done")
        hs_ready, h_ready = sem("hs_ready"), sem("h_ready")
        norm_root, qk_root = sem("norm_root"), sem("qk_root")
        qk_mm, qk_evac, qk_stats, qk_done = sem("qk_mm"), sem("qk_evac"), sem("qk_stats"), sem("qk_done")
        v_mm, v_ready, swapped = sem("v_mm"), sem("v_ready"), sem("swapped")
        p_scaled = sem("p_scaled")
        sc_done, max_ready, exp_done = sem("sc_done"), sem("max_ready"), sem("exp_done")
        p_turned, pt_ready, pv_done, y_evac = sem("p_turned"), sem("pt_ready"), sem("pv_done"), sem("y_evac")
        wo_mm, xw_ready = sem("wo_mm"), sem("xw_ready")
        lg_mm, sig_ready, h_turned, tok_ready = sem("lg_mm"), sem("sig_ready"), sem("h_turned"), sem("tok_ready")
        mask_ready, rank_mm, route_ready = sem("mask_ready"), sem("rank_mm"), sem("route_ready")
        hc_in, hc_turned, hc_ready = per_layer("hc_in"), per_layer("hc_turned"), per_layer("hc_ready")
        gu_mm, silu_done, he_ready = per_layer("gu_mm"), per_layer("silu_done"), per_layer("he_ready")
        he_turned, het_ready, down_mm = per_layer("he_turned"), per_layer("het_ready"), per_layer("down_mm")
        rows_ready, rows_stored = per_layer("rows_ready"), per_layer("rows_stored")
        pos_ready, scattered, rows_all = sem("pos_ready"), sem("scattered"), sem("rows_all")
        yg_in = [[sem(f"yg_in{l}_{t}") for t in range(4)] for l in range(DEPTH)]
        y_scaled, y_summed, c_turned, xc_ready = sem("y_scaled"), sem("y_summed"), sem("c_turned"), sem("xc_ready")
        o_turned, o_act, o_dve, out_done = sem("o_turned"), sem("o_act"), sem("o_dve"), sem("out_done")
        dve_step = sem("dve_step")

        def turned_he(half):
            return bank[(3, 1)[half]][:, 0:256].rearrange("p (k t) -> p k t", k=2)

        def gate_t(half):
            return act_g[:, P * half:P * half + P].rearrange("p (k t) -> p k t", k=2)

        def units(l):
            return [(tt, T, kv, r) for tt in range(TOK_TILES[l]) for T in range(2) for kv in range(2)
                    for r in range(4)]

        def keys(tt):
            return (0, 512) if tt < 2 else (256, 256)

        def expert_weights(e, a):
            return [(3 * a, w_gate, KD), (3 * a + 1, w_up, KD), (3 * a + 2, w_down, KF)]

        def chunks(engine, l, body):
            if CHUNK[l] == SHORT:
                total = engine.value_load(first[0:1, NE:NE + 1], min_val=1, max_val=MAX_CHUNKS[l])
                with engine.Fori(0, total) as g:
                    body(g, SHORT)
            else:
                with engine.Fori(0, NE) as e:
                    expert_chunks(engine, l, e, body)

        def expert_chunks(engine, l, e, body):
            g0 = engine.value_load(first[0:1, bass.ds(e, 1)], min_val=0, max_val=MAX_CHUNKS[l])
            g1 = engine.value_load(first[0:1, bass.ds(e + 1, 1)], min_val=0, max_val=MAX_CHUNKS[l])
            if CHUNK[l] == P:
                gs = engine.value_load(short[0:1, bass.ds(e, 1)], min_val=0, max_val=MAX_CHUNKS[l])
            with engine.Fori(g0, g1) as g:
                if CHUNK[l] == P:
                    with engine.If(g < gs):
                        body(g, P)
                    with engine.Else():
                        body(g, SHORT)
                else:
                    body(g, SHORT)

        block = stack.enter_context(nc.Block())

        @block.sync
        def _(sp):
            def slot(s, k):
                return ring[:, s, :].rearrange("p (k n) -> p k n", k=k)

            def load_ada(s, u, signal):
                l, m = divmod(u, 12)
                sp.dma_start(slot(s, KD), ada_w[l, :, m * 512:m * 512 + 512].rearrange("(k p) n -> p k n", p=P)
                             ).then_inc(signal, 16)

            def load_win(l):
                for q in range(4):
                    sp.dma_start(win[:, 2 * q:2 * q + 2, :],
                                 w_in[l, 256 * q:256 * q + 256, :].rearrange("(k p) n -> p k n", p=P)
                                 ).then_inc(win_in[q], 16)

            def load_wout(l, half):
                sp.dma_start(wout[half], w_out[l, 512 * half:512 * half + 512, :].rearrange("(k p) n -> p k n", p=P)
                             ).then_inc(wout_in[half], 16)

            def load_expert(l, e, a, parts=(0, 1, 2)):
                for part in parts:
                    s, w, k = expert_weights(e, a)[part]
                    src = w[l, bass.ds(e, 1)].rearrange("a (k p) n -> p (a k) n", p=P)
                    sp.dma_start(slot(s, k), src).then_inc(ew_in[l][s], 16)

            sp.dma_start(cst[:, :], table[:, 0:C_END]).then_inc(cst_in, 16)
            sp.dma_start(tokm[:, 0:2, :], x[0].rearrange("(t p) d -> p t d", p=P)).then_inc(x_in, 16)
            sp.dma_start(tokm[:, 2:4, :], ctx_in[0].rearrange("(t p) d -> p t d", p=P)).then_inc(x_in, 16)
            sp.wait_ge(vec_in, 16 * 15)
            for u, s in enumerate((6, 0, 1, 2)):
                load_ada(s, u, ada_in[u])
            load_win(0)
            for part in range(3):
                sp.wait_ge(ada_used, part + 2)
                load_expert(0, 0, 0, (part,))
            for u in range(4, 24):
                if u == 5:
                    sp.wait_ge(v_mm, 2)
                    sp.wait_ge(swapped, 64)
                if u >= 8:
                    sp.wait_ge(ada_used, u - 3)
                load_ada((6, 3, 4, 5)[u % 4], u, ada2_in[u % 4])
            for l in range(DEPTH):
                if l == 0:
                    sp.wait_ge(ada_used, 21)
                    load_wout(0, 0)
                    sp.wait_ge(ada_used, 22)
                    load_wout(0, 1)
                    sp.wait_ge(ada_used, 24)
                else:
                    sp.wait_ge(set_free[0][1], 5)
                    load_win(1)
                    sp.wait_ge(set_free[0][2], 5)
                    load_wout(1, 0)
                    sp.wait_ge(set_free[0][0], 6)
                    sp.wait_ge(yg_in[0][3], 32)
                    load_expert(1, 0, 0)
                    sp.wait_ge(v_mm, 4)
                    sp.wait_ge(swapped, 128)
                    load_wout(1, 1)
                load_expert(l, 1, 1, (1, 2))
                sp.wait_ge(pv_done, sum(UNITS[:l + 1]) // 4)
                load_expert(l, 2, 2, (1, 2))
                sp.wait_ge(wo_mm, KD * (l + 1))
                load_expert(l, 1, 1, (0,))
                load_expert(l, 2, 2, (0,))
                with sp.Fori(1, 5) as i:
                    for a in range(3):
                        sp.wait_ge(set_free[l][a], i)
                        load_expert(l, 3 * i + a, a)
                sp.wait_ge(set_free[l][0], 5)
                load_expert(l, 15, 0)
            for tt in range(2):
                sp.wait_ge(o_act, tt + 1)
                sp.wait_ge(o_dve, tt + 1)
                sp.dma_start(out[0, P * tt:P * tt + P, :], out_tok[:, tt, :]).then_inc(out_done, 16)
            sp.wait_ge(out_done, 32)

        @block.tensor
        def _(pe):
            mm = nc.tensor.matmul
            turn = nc.tensor.transpose

            def ada_unit(u):
                if u < 4:
                    s = (6, 0, 1, 2)[u]
                    pe.wait_ge(ada_in[u], 16)
                else:
                    s = (6, 3, 4, 5)[u % 4]
                    pe.wait_ge(ada2_in[u % 4], 16 * (u // 4))
                if u > 0:
                    pe.wait_ge(parts_ready, u)
                w = ring[:, s, :].rearrange("p (k n) -> p k n", k=KD)
                for k in range(KD):
                    q = k % 4
                    last = mm(bank[7][32 * q:32 * q + 2, :], scv[:, k, :], w[:, k, :],
                              start=(k < 4), stop=(k >= 4))
                last.then_inc(ada_used, 1)

            def ada_turn(u):
                pe.wait_ge(parts_ready, u + 1)
                if u > 0:
                    pe.wait_ge(ada_summed, u)
                for m in range(4):
                    last = turn(bank[2][:, P * m:P * m + P], parts[:, P * m:P * m + P], ident)
                last.then_inc(ada_turned, 1)

            def first_sums():
                for k in range(KD):
                    pe.wait_ge(sq_ready, k + 1)
                    last = mm(bank[0][:, :], ones[:, :], sq[k % 2], start=(k == 0), stop=(k == KD - 1))
                    last.then_inc(sums_done if k == KD - 1 else sq_used, 1)

            def added_sums(l):
                width = P * TOK_TILES[l]
                pe.wait_ge(sq_added, (KD - 1) * (l + 1))
                mm(bank[0][:, 0:width], ones[:, :], rstd[:, 0:width], start=True, stop=True).then_inc(sums_done, 1)

            def tile_sums(tt):
                pe.wait_ge(tile_squared, tt + 1)
                for k in range(KD):
                    last = mm(bank[0][:, P * tt:P * tt + P], ones[:, :], tile_sq[tt][:, k, :],
                              start=(k == 0), stop=(k == KD - 1))
                if tt == TOK_TILES[0] - 1:
                    last.then_inc(sums_done, 1)

            def qk_weights(i, k):
                T, j = divmod(i - 2, 4)
                col = 512 + 768 * i if i < 2 else 768 * T + P * j
                return win[:, k, col:col + P]

            def qk_sums(l, i, n):
                pe.wait_ge(qk_evac, 10 * l + i + 1)
                if 10 * l + i > 1:
                    pe.wait_ge(qk_done, 10 * l + i - 1)
                mm(bank[(3, 0)[i % 2]][:, 0:n], head_ones, sq[i % 2][:, 0:n], start=True, stop=True)
                mm(bank[(4, 7)[i % 2]][:, 0:SEQ], swap, qk_t[:, i, 0:SEQ], start=True, stop=True).then_inc(qk_stats, 1)

            def qkv(l):
                widths = [512, 512] + [P * TOK_TILES[l]] * 8
                for i in range(10):
                    if i >= 2:
                        pe.wait_ge(qk_evac, 10 * l + i - 1)
                    for k in range(KD):
                        if i == 0:
                            pe.wait_ge(h_ready, 2 * KD * l + k + 1)
                            pe.wait_ge(win_in[k // 2], 16 * (l + 1))
                        last = mm(bank[1 + i % 2][:, 0:widths[i]], qk_weights(i, k), h_t[:, k, 0:widths[i]],
                                  start=(k == 0), stop=(k == KD - 1))
                    last.then_inc(qk_mm, 1)
                    if i >= 1:
                        qk_sums(l, i - 1, widths[i - 1])
                for tt in range(4):
                    for k in range(KD):
                        wv = win[:, k, :].rearrange("p (h n) -> p h n", h=2)[:, :, 640:768]
                        o = bank[5 + tt // 2][:, 256 * (tt % 2):256 * (tt % 2) + 256].rearrange("p (h n) -> p h n", h=2)
                        last = mm(o, h_t[:, k, P * tt:P * tt + P], wv, start=(k == 0), stop=(k == KD - 1))
                    if tt % 2:
                        last.then_inc(v_mm, 1)
                    if tt == 0:
                        qk_sums(l, 9, widths[9])

            def attention(l):
                ub, gb = sum(UNITS[:l]), sum(UNITS[:l]) // 4
                us = units(l)

                def scores(n):
                    tt, T, kv, r = us[n]
                    k0, kn = keys(tt)
                    if n == 0:
                        pe.wait_ge(qk_done, 10 * (l + 1))
                        pe.wait_ge(swapped, 64 * (l + 1))
                    if n >= 2:
                        pe.wait_ge(exp_done, ub + n - 1)
                    a = r % 2
                    rows = slice(HD * a, HD * a + HD)
                    k_t = (qk_t[:, T] if a == kv else sq[T])[rows, k0:k0 + kn]
                    q_t = qk_t[rows, 2 + 4 * T + 2 * kv + r // 2, P * tt:P * tt + P]
                    o = bank[n % 2]
                    parts = [(0, kn, False)]
                    if T == 1 and tt < 2:
                        parts = ([(0, P, False), (P, 2 * P, True), (2 * P, kn, False)] if tt == 0 else
                                 [(0, P, True), (P, kn, False)])
                    for c0, c1, masked in parts:
                        last = mm(o[:, c0:c1], q_t, k_t[:, c0:c1], start=True, stop=not masked)
                        if masked:
                            last = mm(o[:, c0:c1], ident, band[tt], start=False, stop=True)
                    last.then_inc(sc_done, 1)

                def turn_probs(n):
                    tt = us[n][0]
                    pe.wait_ge(p_scaled, ub + n + 1)
                    if n >= 2:
                        pe.wait_ge(pt_ready, ub + n - 1)
                    for q in range(keys(tt)[1] // P):
                        last = turn(bank[4 + n % 2][:, P * q:P * q + P], probs[:, n % 4, P * q:P * q + P], ident)
                    last.then_inc(p_turned, 1)

                def values(g):
                    tt, T, kv, _ = us[4 * g]
                    k0, kn = keys(tt)
                    pe.wait_ge(pt_ready, ub + 4 * g + 4)
                    if g == 0:
                        pe.wait_ge(v_ready, 2 * (l + 1))
                    if g >= 2:
                        pe.wait_ge(y_evac, gb + g - 1)
                    nk = kn // P
                    col = P * T + HD * kv
                    for q in range(nk):
                        for odd in range(2):
                            last = mm(bank[(3, 6)[g % 2]][HD * odd:HD * odd + HD, 0:256],
                                      v_tok[:, k0 // P + q, col:col + HD],
                                      probs_t[:, q, 256 * odd:256 * odd + 256], start=(q == 0), stop=(q == nk - 1))
                    last.then_inc(pv_done, 1)

                for n in range(UNITS[l] + 4):
                    if n < UNITS[l]:
                        scores(n)
                    if n >= 6 and n % 4 == 2:
                        values(n // 4 - 1)
                    if 2 <= n < UNITS[l] + 2:
                        turn_probs(n - 2)
                    if l == 0 and n % 3 == 1 and n // 3 < 20:
                        ada_unit(4 + n // 3)
                    if l == 0 and n % 3 == 2 and n // 3 < 20:
                        ada_turn(4 + n // 3)

            def project_out(l):
                nt = TOK_TILES[l]
                pe.wait_ge(y_evac, sum(UNITS[:l + 1]) // 4)
                for m in range(KD):
                    if m >= 2:
                        pe.wait_ge(xw_ready, KD * l + m - 1)
                    for k in range(KD):
                        if m == 0:
                            pe.wait_ge(wout_in[k // 4], 16 * (l + 1))
                        last = mm(bank[4 + m % 2][:, 0:P * nt], wout[k // 4][:, k % 4, P * m:P * m + P],
                                  y_t[:, k, 0:P * nt], start=(k == 0), stop=(k == KD - 1))
                    last.then_inc(wo_mm, 1)

            def route(l):
                nt = TOK_TILES[l]
                tb = 2 * sum(TOK_TILES[:l])
                for tt in range(nt):
                    for k in range(KD):
                        if tt == 0:
                            pe.wait_ge(h_ready, KD * (2 * l + 1) + k + 1)
                        last = mm(bank[1][:, NE * tt:NE * tt + NE], h_t[:, k, P * tt:P * tt + P], rw[:, k, :],
                                  start=(k == 0), stop=(k == KD - 1))
                last.then_inc(lg_mm, 1)
                for q in range(2 * nt):
                    if q >= 4:
                        pe.wait_ge(tok_ready, tb + q - 3)
                    for k in range(4):
                        kk = 4 * (q % 2) + k
                        last = turn(bank[2 + q % 4][:, P * k:P * k + P], h_t[:, kk, P * (q // 2):P * (q // 2) + P], ident)
                    last.then_inc(h_turned, 1)
                pe.wait_ge(mask_ready, l + 1)
                mask = mask_b[:, 0:NE * nt].rearrange("p (t e) -> p t e", t=nt)
                for tt in range(nt):
                    for t2 in range(tt + 1):
                        mm(bank[6][:, NE * tt:NE * tt + NE], upper_b[:, :] if t2 == tt else ones_b[:, :], mask[:, t2, :],
                           start=(t2 == 0), stop=(t2 == tt))
                for t2 in range(nt):
                    last = mm(bank[6][:, NE * nt:NE * nt + NE], ones_b[:, :], mask[:, t2, :],
                              start=(t2 == 0), stop=(t2 == nt - 1))
                last.then_inc(rank_mm, 1)

            def experts(l):
                def turn_rows(n):
                    pe.wait_ge(hc_in[l], 16 * n + 16)
                    for k in range(KD):
                        last = turn(bank[5 + k // 4][:, P * (k % 4):P * (k % 4) + P], hc[:, P * k:P * k + P], ident)
                    last.then_inc(hc_turned[l], 1)

                def gate_up(half, w, rows):
                    for s, k in ([(s, k) for s in range(2) for k in range(KD)] if rows == P else
                                 [(s, k) for k in range(KD) for s in range(2)]):
                        o = (bank[1 + half][:, 256 * s:256 * s + 256] if rows == P else
                             bank[1 + half][rows * s:rows * s + rows, 0:256])
                        last = mm(o, hc_t[:, k, 0:rows], w[s][:, k, 256 * half:256 * half + 256],
                                  start=(k == 0), stop=(k == KD - 1))
                    last.then_inc(gu_mm[l], 1)

                def chunk(a, turns, g, rows):
                    w = [ring[:, 3 * a + s, :].rearrange("p (k n) -> p k n", k=KD) for s in range(2)]
                    wd = ring[:, 3 * a + 2, :].rearrange("p (k n) -> p k n", k=KF)
                    pe.wait_ge(hc_ready[l], g + 1)
                    pe.wait_ge(ew_in[l][3 * a], 16 * turns)
                    pe.wait_ge(ew_in[l][3 * a + 1], 16 * turns)
                    for half in range(2):
                        gate_up(half, w, rows)
                    turn_rows(g + 1)
                    for half in range(2):
                        pe.wait_ge(he_ready[l], 2 * g + 1 + half)
                        for q in range(2):
                            last = turn(bank[(3, 1)[half]][:, P * q:P * q + P],
                                        he[:, 256 * half + P * q:256 * half + P * q + P], ident)
                        last.then_inc(he_turned[l], 1)
                    pe.wait_ge(ew_in[l][3 * a + 2], 16 * turns)
                    pe.wait_ge(rows_ready[l], g + 1)
                    for k in range(KF):
                        if k % 2 == 0:
                            pe.wait_ge(het_ready[l], 2 * g + 1 + k // 2)
                        for n in range(2):
                            o = bank[(4, 7)[n]][:, :] if rows == P else bank[4][rows * n:rows * n + rows, :]
                            last = mm(o, he_t[:, k, 0:rows], wd[:, k, 512 * n:512 * n + 512],
                                      start=(k == 0), stop=(k == KF - 1))
                    last.then_inc(down_mm[l], 1)

                def expert(e, a, turns):
                    expert_chunks(pe, l, e, lambda g, rows: chunk(a, turns, g, rows))
                    mm(bank[0][:, 0:1], ones[:, :], ones[:, 0:1], start=True, stop=True).then_inc(set_free[l][a], 1)

                pe.wait_ge(route_ready, l + 1)
                turn_rows(0)
                with pe.Fori(0, 5) as i:
                    for a in range(3):
                        expert(3 * i + a, a, i + 1)
                expert(15, 0, 6)

            def combine(l):
                nt = TOK_TILES[l]
                tb = sum(TOK_TILES[:l])
                for tt in range(nt):
                    pe.wait_ge(y_summed, tb + tt + 1)
                    if tt >= 2:
                        pe.wait_ge(xc_ready, tb + tt - 1)
                    for k in range(KD):
                        last = turn(bank[1 + 2 * (tt % 2) + k // 4][:, P * (k % 4):P * (k % 4) + P],
                                    tokm[:, tt, P * k:P * k + P], ident)
                    last.then_inc(c_turned, 1)
                    if l == 0 and tt >= 2:
                        tile_sums(tt - 2)
                if l == 0:
                    tile_sums(nt - 2)
                    tile_sums(nt - 1)

            pe.wait_ge(cst_in, 16)
            pe.wait_ge(vec_in, 16 * 15)
            turn(bank[0][:, 0:96], vec_a, ident[0:96, 0:96])
            turn(bank[0][:, 96:V_END], vec_b, ident[0:V_END - 96, 0:V_END - 96]).then_inc(vec_turned, 1)
            pe.wait_ge(x_in, 32)
            for k in range(KD):
                if k >= 6:
                    pe.wait_ge((xt_act, xt_dve)[k % 2], 1)
                for tt in range(4):
                    last = turn(bank[1 + k % 6][:, P * tt:P * tt + P], tokm[:, tt, P * k:P * k + P], ident)
                last.then_inc(x_turned, 1)
            pe.wait_ge(ones_set, 1)
            pe.wait_ge(silu_ready, 1)
            pe.wait_ge(bank7_set, 1)
            for l in range(DEPTH):
                if l == 0:
                    first_sums()
                    for u in range(4):
                        ada_unit(u)
                        ada_turn(u)
                qkv(l)
                attention(l)
                project_out(l)
                added_sums(l)
                if l == 0:
                    pe.wait_ge(small_in, 32)
                route(l)
                experts(l)
                combine(l)
            pe.wait_ge(xc_ready, sum(TOK_TILES))
            for tt in range(2):
                for k in range(KD):
                    last = turn(bank[(5, 6, 0, 7)[2 * tt + k // 4]][:, P * (k % 4):P * (k % 4) + P],
                                x_t[:, k, P * tt:P * tt + P], ident)
                last.then_inc(o_turned, 1)

        @block.scalar
        def _(act):
            do = nc.scalar.activation

            def first_squares():
                for k in range(KD):
                    act.wait_ge((xt_act, xt_dve)[k % 2], k // 2 + 1)
                    if k >= 2:
                        act.wait_ge(sq_used, k - 1)
                    do(sq[k % 2], x_t[:, k, :], ACT.Square).then_inc(sq_ready, 1)

            def squares(l):
                width = P * TOK_TILES[l]
                for k in range(KD):
                    act.wait_ge(xw_ready, KD * l + k + 1)
                    if k >= 3:
                        act.wait_ge(sq_added, (KD - 1) * l + k - 2)
                    do((sq[k % 2] if k else rstd)[:, 0:width], x_t[:, k, 0:width], ACT.Square
                       ).then_inc(sq_ready, 1)

            def tile_squares(tt):
                act.wait_ge(xc_ready, tt + 1)
                do(tile_sq[tt], x_t[:, :, P * tt:P * tt + P], ACT.Square).then_inc(tile_squared, 1)

            def norm_roots(n, width):
                act.wait_ge(sums_done, n + 1)
                do(rstd[:, 0:width], bank[0][:, 0:width], ACT.Sqrt, bias=eps[:, 0:1]).then_inc(norm_root, 1)

            def norm_shift(n, width):
                l, w = divmod(n, 2)
                for k in range(KD):
                    act.wait_ge(hs_ready, KD * n + k + 1)
                    for src in range(width // 256):
                        m = l * NMOD + 3 * KD * w + k
                        cols = slice(256 * src, 256 * src + 256)
                        last = do(h_t[:, k, cols], h_t[:, k, cols], ACT.Identity, bias=mods[:, m, src:src + 1])
                    last.then_inc(h_ready, 1)

            def qkv(l):
                widths = [512, 512] + [P * TOK_TILES[l]] * 8

                def root(i):
                    act.wait_ge(qk_stats, 10 * l + i + 1)
                    if 10 * l + i > 0:
                        act.wait_ge(qk_done, 10 * l + i)
                    do(rstd[:, 0:widths[i]], bank[(3, 0)[i % 2]][:, 0:widths[i]], ACT.Sqrt, bias=eps[:, 1:2]).then_inc(qk_root, 1)

                for i in range(10):
                    n = widths[i]
                    act.wait_ge(qk_mm, 10 * l + i + 1)
                    if i >= 2:
                        act.wait_ge(qk_stats, 10 * l + i - 1)
                    do(sq[i % 2][:, 0:n], bank[1 + i % 2][:, 0:n], ACT.Square)
                    kind = (1, 3)[i] if i < 2 else 2 * ((i - 2) // 4)
                    col = V_QN + DEPTH * kind + l
                    do(qk_t[:, i, 0:n], bank[1 + i % 2][:, 0:n], ACT.Identity,
                       scale=vec[:, col:col + 1]).then_inc(qk_evac, 1)
                    if i >= 1:
                        root(i - 1)
                root(9)
                for q in range(2):
                    act.wait_ge(v_mm, 2 * l + q + 1)
                    do(v_tok[:, 2 * q:2 * q + 2, :].rearrange("p t n -> p (t n)"), bank[5 + q][:, :],
                       ACT.Identity).then_inc(v_ready, 1)

            def ada_parts(u):
                act.wait_ge(ada_used, u + 1)
                if u > 0:
                    act.wait_ge(ada_turned, u)
                do(parts, bank[7][:, :], ACT.Identity).then_inc(parts_ready, 1)

            def attention(l):
                ub, gb = sum(UNITS[:l]), sum(UNITS[:l]) // 4
                us = units(l)

                def exponentials(n):
                    tt, T, kv, r = us[n]
                    kn = keys(tt)[1]
                    head = l * 8 + 4 * kv + r
                    act.wait_ge(max_ready, ub + n + 1)
                    if n >= 4:
                        act.wait_ge(p_turned, ub + n - 3)
                    if T:
                        do(esink[:, n:n + 1], sink[:, head:head + 1], ACT.Exp, bias=negmax[:, n:n + 1])
                    do(probs[:, n % 4, 0:kn], bank[n % 2][:, 0:kn], ACT.Exp, bias=negmax[:, n:n + 1], scale=SCALE,
                       accum_out=lsum[:, n:n + 1]).then_inc(exp_done, 1)

                def probs_out(n):
                    nk = keys(us[n][0])[1] // P
                    g, r = divmod(n, 4)
                    act.wait_ge(p_turned, ub + n + 1)
                    if r == 0 and g >= 1:
                        act.wait_ge(pv_done, gb + g)
                    col = 256 * (r % 2) + P * (r // 2)
                    do(probs_t[:, 0:nk, col:col + P], bank[4 + n % 2][:, 0:P * nk].rearrange("p (k q) -> p k q", k=nk),
                       ACT.Identity).then_inc(pt_ready, 1)

                for n in range(UNITS[l] + 2):
                    if n < UNITS[l]:
                        exponentials(n)
                    if n >= 2:
                        probs_out(n - 2)
                    if l == 0 and n % 3 == 1 and n // 3 < 20:
                        ada_parts(4 + n // 3)

            def route(l):
                nt = TOK_TILES[l]
                act.wait_ge(lg_mm, l + 1)
                do(work[:, 512:512 + NE * nt], bank[1][:, 0:NE * nt], ACT.Sigmoid).then_inc(sig_ready, 1)
                for q in range(2 * nt):
                    act.wait_ge(h_turned, 2 * sum(TOK_TILES[:l]) + q + 1)
                    do(tokm[:, q // 2, 512 * (q % 2):512 * (q % 2) + 512], bank[2 + q % 4][:, :],
                       ACT.Identity).then_inc(tok_ready, 1)

            def experts(l):
                def chunk_turned(n):
                    act.wait_ge(hc_turned[l], n + 1)
                    do(hc_t[:, 0:4, :].rearrange("p k t -> p (k t)"), bank[5][:, :], ACT.Identity)
                    do(hc_t[:, 4:8, :].rearrange("p k t -> p (k t)"), bank[6][:, :],
                       ACT.Identity).then_inc(hc_ready[l], 1)

                def chunk(g, rows):
                    for half in range(2):
                        if rows == P:
                            act.wait_ge(gu_mm[l], 2 * g + 1 + half)
                            do(act_g[:, 256 * half:256 * half + 256], bank[1 + half][:, 0:256],
                               ACT.Silu).then_inc(silu_done[l], 1)
                        else:
                            act.wait_ge(he_turned[l], 2 * g + 1 + half)
                            do(gate_t(half), turned_he(half)[:, :, 0:rows], ACT.Silu).then_inc(silu_done[l], 1)
                    chunk_turned(g + 1)
                    act.wait_ge(down_mm[l], g + 1)
                    act.wait_ge(rows_stored[l], 32 * g + 16)
                    last = do(yrow[:, 0:512], bank[4][:, :], ACT.Identity)
                    if rows == P:
                        last = do(yrow[:, 512:D], bank[7][:, :], ACT.Identity)
                    last.then_inc(rows_ready[l], 1)

                act.wait_ge(route_ready, l + 1)
                chunk_turned(0)
                chunks(act, l, chunk)

            def combine(l):
                for tt in range(TOK_TILES[l]):
                    act.wait_ge(yg_in[l][tt], 32)
                    do(ych[0][:, tt, :], ych[0][:, tt, :], ACT.Identity,
                       scale=wgt[:, tt:tt + 1]).then_inc(y_scaled, 1)
                    if l == 0 and tt >= 2:
                        tile_squares(tt - 2)
                if l == 0:
                    tile_squares(2)
                    tile_squares(3)

            act.dma_start(vec_a, ada_b.rearrange("l (m p) -> (l m) p", p=P)).then_inc(vec_in, 16)

            def vec_rows(row, n, cols, src):
                r = row - 96
                act.dma_start(h_t[r:r + n, 0, P + cols[0]:P + cols[1]], src).then_inc(vec_in, 16)

            vec_rows(V_AG, DEPTH * KD, (0, P), attn_norm_g.rearrange("l (k p) -> (l k) p", p=P))
            vec_rows(V_FG, DEPTH * KD, (0, P), ffn_norm_g.rearrange("l (k p) -> (l k) p", p=P))
            vec_rows(V_C, KD, (0, P), c.rearrange("b (k p) -> (b k) p", p=P))
            vec_rows(V_CC, KD, (0, P), c_ctx.rearrange("(k p) -> k p", p=P))
            for i, g in enumerate((qn_global, kn_global, qn_local, kn_local)):
                for half in range(2):
                    vec_rows(V_QN + DEPTH * i, DEPTH, (HD * half, HD * half + HD), g)
            act.dma_start(sink[:, :], sink_logit.rearrange("l h -> (l h)").partition_broadcast(P)
                          ).then_inc(vec_in, 16)
            act.dma_start(upper_f, table[:, C_UP:C_ALL]).then_inc(vec_in, 16)
            act.dma_start(rb[:, :], router_b.partition_broadcast(P)).then_inc(small_in, 16)
            act.dma_start(rw[:, :, :], router_w.rearrange("(k p) e -> p k e", p=P)).then_inc(small_in, 16)

            act.wait_ge(vec_ready, 1)
            do(scv[:, :, 0], vec[:, V_C:V_C + KD], ACT.Silu)
            do(scv[:, :, 1], vec[:, V_CC:V_CC + KD], ACT.Silu).then_inc(silu_ready, 1)
            for k in range(0, KD, 2):
                act.wait_ge(x_turned, k + 1)
                do(x_t[:, k, :], bank[1 + k % 6][:, :], ACT.Identity).then_inc(xt_act, 1)
            for l in range(DEPTH):
                if l == 0:
                    for stored in rows_stored:
                        act.wait_ge(stored, 16)
                    first_squares()
                norm_roots(2 * l, 512)
                if l == 0:
                    for u in range(4):
                        ada_parts(u)
                norm_shift(2 * l, 512)
                qkv(l)
                attention(l)
                squares(l)
                norm_roots(2 * l + 1, P * TOK_TILES[l])
                norm_shift(2 * l + 1, P * TOK_TILES[l])
                route(l)
                experts(l)
                combine(l)
            for tt in range(2):
                act.wait_ge(o_turned, tt + 1)
                do(out_tok[:, tt, 0:512], bank[(5, 0)[tt]][:, :], ACT.Identity).then_inc(o_act, 1)

        @block.gpsimd
        def _(pool):
            pool.wait_ge(rows_ready[0], 1)
            for l, rows_dram in enumerate((h_rows, y_rows)):
                pool.dma_start(rows_dram[ROWS:ROWS + P, :], yrow).then_inc(rows_stored[l], 16)
            for l in range(DEPTH):
                nt = TOK_TILES[l]
                rows = CHUNK[l]
                pool.wait_ge(qk_done, 10 * (l + 1))
                for T in range(2):
                    for a in range(2):
                        pool.dma_start(sq[T][HD * a:HD * a + HD, :], qk_t[HD * (1 - a):HD * (2 - a), T, :]
                                       ).then_inc(swapped, 16)
                pool.wait_ge(tok_ready, 2 * sum(TOK_TILES[:l + 1]))
                pool.wait_ge(pos_ready, l + 1)
                for tt in range(nt):
                    for s in range(2):
                        pool.indirect_dma_start(h_rows[0:2 * nt * P, :],
                                                bass.IndirectOffsetOnAxis(posidx[:, nt * s + tt:nt * s + tt + 1], 0),
                                                tokm[:, tt, :], None).then_inc(scattered, 16)
                pool.wait_ge(scattered, 32 * sum(TOK_TILES[:l + 1]))
                pool.wait_ge(rows_stored[l], 16)
                pool.wait_ge(route_ready, l + 1)

                def row_of(n):
                    return pool.value_load(chunk_row[0:1, bass.ds(n, 1)], min_val=0, max_val=ROWS)

                def load_rows(n):
                    pool.dma_start(hc[0:rows, :], h_rows[bass.ds(row_of(n), rows), :]).then_inc(hc_in[l], 16)

                load_rows(0)
                pool.wait_ge(hc_turned[l], 1)
                load_rows(1)

                def chunk(g, rows):
                    pool.wait_ge(hc_turned[l], g + 2)
                    load_rows(g + 2)
                    pool.wait_ge(rows_ready[l], g + 2)
                    row = row_of(g)
                    for s in range(2):
                        src = yrow[:, 512 * s:512 * s + 512] if rows == P else yrow[rows * s:rows * s + rows, 0:512]
                        pool.dma_start(y_rows[bass.ds(row, rows), 512 * s:512 * s + 512], src
                                       ).then_inc(rows_stored[l], 16)

                chunks(pool, l, chunk)
                total = pool.value_load(first[0:1, NE:NE + 1], min_val=1, max_val=MAX_CHUNKS[l])
                pool.wait_ge(rows_stored[l], total * 32 + 16)
                pool.wait_ge(hc_in[l], total * 16 + 32)
                pool.sem_inc(rows_all, 1)
                pool.wait_ge(rows_all, l + 1)
                for tt in range(nt):
                    for s in range(2):
                        pool.indirect_dma_start(ych[s][:, tt, :], None, y_rows[0:2 * nt * P, :],
                                                bass.IndirectOffsetOnAxis(posidx[:, nt * s + tt:nt * s + tt + 1], 0)
                                                ).then_inc(yg_in[l][tt], 16)

        @block.vector
        def _(dve):
            v = nc.vector
            chain = [0]

            def link(ins):
                chain[0] += 1
                ins.then_inc(dve_step, 1)
                dve.wait_ge(dve_step, chain[0])

            def gains(l):
                for w in range(2):
                    m = l * NMOD + (3 * w + 1) * KD
                    g0 = (V_AG, V_FG)[w] + l * KD
                    link(v.tensor_scalar(gain[:, l, w], mods[:, m:m + KD, :], 1.0, D ** 0.5, ALU.add, ALU.mult))
                    gv = vec[:, g0:g0 + KD].unsqueeze(2).to_broadcast([P, KD, 2])
                    link(v.tensor_tensor(gain[:, l, w], gain[:, l, w], gv, ALU.mult))

            def ada_sum(u):
                dve.wait_ge(ada_turned, u + 1)
                ps = bank[2][:, :].rearrange("p (m q x) -> p m x q", m=4, q=4)[:, :, 0:2, :]
                v.tensor_reduce(mods[:, 4 * u:4 * u + 4, :], ps, AX.X, ALU.add).then_inc(ada_summed, 1)

            def add_bias(m0, m1):
                dve.wait_ge(ada_summed, m1 // 4)
                bias = vec[:, V_ADAB + m0:V_ADAB + m1].unsqueeze(2).to_broadcast([P, m1 - m0, 2])
                link(v.tensor_tensor(mods[:, m0:m1, :], mods[:, m0:m1, :], bias, ALU.add))

            def norm_scale(n, width):
                l, w = divmod(n, 2)
                dve.wait_ge(norm_root, n + 1)
                link(v.reciprocal(rstd[:, 0:width], rstd[:, 0:width]))
                for k in range(KD):
                    for src in range(width // 256):
                        cols = slice(256 * src, 256 * src + 256)
                        last = v.scalar_tensor_tensor(out=h_t[:, k, cols], in0=x_t[:, k, cols],
                                                      scalar=gain[:, l, w, k, src:src + 1], in1=rstd[:, cols],
                                                      op0=ALU.mult, op1=ALU.mult)
                    last.then_inc(hs_ready, 1)

            def qk_norms(l):
                widths = [512, 512] + [P * TOK_TILES[l]] * 8
                for i in range(10):
                    n = widths[i]
                    dve.wait_ge(qk_root, 10 * l + i + 1)
                    v.reciprocal(rstd[:, 0:n], rstd[:, 0:n])
                    v.tensor_tensor(rope_a, qk_t[:, i, 0:SEQ], cos, ALU.mult)
                    link(v.tensor_tensor(rope_b, bank[(4, 7)[i % 2]][:, 0:SEQ], sin, ALU.mult))
                    link(v.tensor_tensor(qk_t[:, i, 0:SEQ], rope_a, rope_b, ALU.add))
                    v.scalar_tensor_tensor(out=qk_t[:, i, 0:n], in0=qk_t[:, i, 0:n], scalar=float(HD ** 0.5),
                                           in1=rstd[:, 0:n], op0=ALU.mult, op1=ALU.mult).then_inc(qk_done, 1)
                    dve.wait_ge(qk_done, 10 * l + i + 1)

            def attention(l):
                ub, gb = sum(UNITS[:l]), sum(UNITS[:l]) // 4
                us = units(l)
                nu = UNITS[l]
                dve.wait_ge(v_mm, 2 * (l + 1))
                link(v.memset(esink[:, 0:nu], 0.0))

                def maxima(n):
                    tt, T, kv, r = us[n]
                    head = l * 8 + 4 * kv + r
                    dve.wait_ge(sc_done, ub + n + 1)
                    link(v.tensor_reduce(smx[:, n:n + 1], bank[n % 2][:, 0:keys(tt)[1]], AX.X, ALU.max))
                    if T:
                        ins = v.tensor_scalar(negmax[:, n:n + 1], smx[:, n:n + 1], -SCALE, nsink[:, head:head + 1],
                                              ALU.mult, ALU.min)
                    else:
                        ins = v.tensor_scalar(negmax[:, n:n + 1], smx[:, n:n + 1], -SCALE, None, ALU.mult)
                    ins.then_inc(max_ready, 1)

                def scale_probs(n):
                    kn = keys(us[n][0])[1]
                    dve.wait_ge(exp_done, ub + n + 1)
                    if us[n][1]:
                        link(v.tensor_tensor(lsum[:, n:n + 1], lsum[:, n:n + 1], esink[:, n:n + 1], ALU.add))
                    link(v.reciprocal(lrec[:, n:n + 1], lsum[:, n:n + 1]))
                    v.tensor_scalar(probs[:, n % 4, 0:kn], probs[:, n % 4, 0:kn], lrec[:, n:n + 1], None,
                                    ALU.mult).then_inc(p_scaled, 1)

                def y_out(g):
                    tt, T, kv, _ = us[4 * g]
                    dve.wait_ge(pv_done, gb + g + 1)
                    k = 4 * T + 2 * kv
                    v.tensor_copy(y_t[:, k:k + 2, P * tt:P * tt + P],
                                  bank[(3, 6)[g % 2]][:, 0:256].rearrange("p (i q) -> p i q", i=2)).then_inc(y_evac, 1)

                for n in range(nu + 4):
                    if n < nu:
                        maxima(n)
                    if 1 <= n < nu + 1:
                        scale_probs(n - 1)
                    if n >= 7 and n % 4 == 3:
                        y_out(n // 4 - 1)
                    if l == 0 and n % 3 == 2 and n // 3 < 20:
                        ada_sum(4 + n // 3)

            def add_attention(l):
                width = P * TOK_TILES[l]

                def add_squares(k):
                    dve.wait_ge(sq_ready, KD * (l + 1) + k + 1)
                    v.tensor_tensor(rstd[:, 0:width], rstd[:, 0:width], sq[k % 2][:, 0:width], ALU.add
                                    ).then_inc(sq_added, 1)
                    dve.wait_ge(sq_added, (KD - 1) * l + k)

                for m in range(KD):
                    dve.wait_ge(wo_mm, KD * l + m + 1)
                    for src in range(TOK_TILES[l] // 2):
                        cols = slice(256 * src, 256 * src + 256)
                        mod = l * NMOD + 2 * KD + m
                        last = v.scalar_tensor_tensor(out=x_t[:, m, cols], in0=bank[4 + m % 2][:, cols],
                                                      scalar=mods[:, mod, src:src + 1], in1=x_t[:, m, cols],
                                                      op0=ALU.mult, op1=ALU.add)
                    last.then_inc(xw_ready, 1)
                    if m >= 2:
                        add_squares(m - 1)
                add_squares(KD - 1)

            def route(l):
                nt = TOK_TILES[l]
                n16 = NE * nt
                rows = float(CHUNK[l])
                thr = C_THR + l * (MAXCH - 1)

                def tmp(i):
                    return work[:, 64 * i:64 * i + n16]

                def te(a):
                    return a.rearrange("p (t e) -> p t e", t=nt)

                eq, sel, oh1, oh2, cand, rank = (tmp(i) for i in (1, 2, 3, 4, 5, 6))
                mask = mask_b[:, 0:n16]
                sc = work[:, 512:512 + n16]
                hi = work[:, 576:576 + 8 * nt]
                lo = work[:, 608:608 + 8 * nt]
                g4 = [work[:, 640 + 16 * i:640 + 16 * i + 4 * nt] for i in range(5)]
                t1 = [work[:, 720 + 4 * i:720 + 4 * i + nt] for i in range(4)]
                tot = work[:, 768:768 + NE]
                nch = work[:, 784:784 + NE]
                firstf = work[:, 800:800 + NE + 1]
                cmp = work[:, 832:832 + NE * (MAXCH - 1)]
                tri = work[:, 960:960 + NE * (NE + 1)]
                base = work[:, 880:880 + NE + 1]
                lastf = work[:, 928:928 + NE]
                rowf = work[:, 900:900 + GT]
                owns = [hflat[:, 1024 + 512 * i:1024 + 512 * i + GT * NE].rearrange("p (g e) -> p g e", e=NE)
                        for i in range(2)]

                def per_tile(a, n):
                    return a.unsqueeze(2).to_broadcast([P, nt, n])

                def best(values, order, n, hot, e4, c4):
                    link(v.tensor_reduce(t1[0], values, AX.X, ALU.max))
                    link(v.tensor_tensor(e4, values, per_tile(t1[0], n), ALU.is_equal))
                    link(v.tensor_tensor(c4, e4, order.unsqueeze(1).to_broadcast([P, nt, n]), ALU.mult))
                    link(v.tensor_reduce(t1[0], c4, AX.X, ALU.max))
                    link(v.tensor_tensor(hot, c4, per_tile(t1[0], n), ALU.is_equal))

                dve.wait_ge(sig_ready, l + 1)
                if l == 0:
                    dve.wait_ge(small_in, 32)
                link(v.tensor_tensor(te(sel), te(sc), rb[:, :].unsqueeze(1).to_broadcast([P, nt, NE]), ALU.add))
                pair = sel.rearrange("p (g j i) -> p g j i", j=2, i=2)
                hi3 = hi.rearrange("p (g j) -> p g j", j=2)
                lo3 = lo.rearrange("p (g j) -> p g j", j=2)
                v.tensor_tensor(hi3, pair[:, :, :, 0], pair[:, :, :, 1], ALU.max)
                link(v.tensor_tensor(lo3, pair[:, :, :, 0], pair[:, :, :, 1], ALU.min))
                v.tensor_tensor(g4[0], hi3[:, :, 0], hi3[:, :, 1], ALU.max)
                v.tensor_tensor(g4[1], hi3[:, :, 0], hi3[:, :, 1], ALU.min)
                link(v.tensor_tensor(g4[2], lo3[:, :, 0], lo3[:, :, 1], ALU.max))
                link(v.tensor_tensor(g4[1], g4[1], g4[2], ALU.max))
                link(v.tensor_tensor(g4[0], g4[0], g4[1], ALU.add))
                tg = [a.rearrange("p (t g) -> p t g", t=nt) for a in g4]
                best(tg[0], cst[:, C_W4:C_W4 + NG], NG, tg[3], tg[1], tg[2])
                link(v.tensor_scalar(g4[4], g4[3], 1.0, BIG, ALU.subtract, ALU.mult))
                link(v.tensor_tensor(sel.rearrange("p (g i) -> p g i", i=EPG), sel.rearrange("p (g i) -> p g i", i=EPG),
                                     g4[4].unsqueeze(2).to_broadcast([P, NG * nt, EPG]), ALU.add))
                best(te(sel), cst[:, C_W16:C_W16 + NE], NE, te(oh1), te(eq), te(cand))
                link(v.scalar_tensor_tensor(out=sel, in0=oh1, scalar=-3e38, in1=sel, op0=ALU.mult, op1=ALU.add))
                best(te(sel), cst[:, C_W16:C_W16 + NE], NE, te(oh2), te(eq), te(cand))
                v.tensor_tensor(mask, oh1, oh2, ALU.add).then_inc(mask_ready, 1)
                dve.wait_ge(rank_mm, l + 1)
                v.tensor_copy(rank, bank[6][:, 0:n16])
                link(v.tensor_copy(tot, bank[6][:, n16:n16 + NE]))
                fe = cst[:, C_TRI:C_THR].rearrange("p (f e) -> p f e", e=NE)
                tri3 = tri.rearrange("p (f e) -> p f e", e=NE)
                link(v.tensor_tensor(tri3, tot.unsqueeze(1).to_broadcast([P, NE + 1, NE]), fe, ALU.mult))
                link(v.tensor_reduce(base, tri3, AX.X, ALU.add))
                link(v.tensor_tensor(te(rank), te(rank), base[:, 0:NE].unsqueeze(1).to_broadcast([P, nt, NE]), ALU.add))
                for s, oh in enumerate((oh1, oh2)):
                    link(v.tensor_tensor(eq, oh, rank, ALU.mult))
                    link(v.tensor_reduce(pos[:, nt * s:nt * s + nt], te(eq), AX.X, ALU.add))
                v.tensor_copy(posidx[:, 0:2 * nt], pos[:, 0:2 * nt]).then_inc(pos_ready, 1)
                weights(l)
                link(v.tensor_tensor(cmp.rearrange("p (e j) -> p e j", e=NE), tot.unsqueeze(2).to_broadcast([P, NE, MAXCH - 1]),
                                     cst[:, thr:thr + MAXCH - 1].unsqueeze(1).to_broadcast([P, NE, MAXCH - 1]), ALU.is_gt))
                link(v.tensor_reduce(nch, cmp.rearrange("p (e j) -> p e j", e=NE), AX.X, ALU.add))
                link(v.tensor_scalar(nch, nch, 1.0, None, ALU.add))
                link(v.tensor_tensor(tri3, nch.unsqueeze(1).to_broadcast([P, NE + 1, NE]), fe, ALU.mult))
                link(v.tensor_reduce(firstf, tri3, AX.X, ALU.add))
                v.tensor_copy(first[:, :], firstf)
                if l == 0:
                    link(v.scalar_tensor_tensor(out=lastf, in0=nch, scalar=-rows, in1=tot, op0=ALU.mult, op1=ALU.add))
                    link(v.tensor_scalar(lastf, lastf, float(SHORT) - rows, None, ALU.is_le))
                    link(v.tensor_tensor(short[:, :], firstf[:, 1:NE + 1], lastf, ALU.subtract))
                link(v.scalar_tensor_tensor(out=base[:, 0:NE], in0=firstf[:, 0:NE], scalar=-rows,
                                            in1=base[:, 0:NE], op0=ALU.mult, op1=ALU.add))
                gs = cst[:, C_G:C_G + GT].unsqueeze(2).to_broadcast([P, GT, NE])
                v.tensor_tensor(owns[0], gs, firstf[:, 0:NE].unsqueeze(1).to_broadcast([P, GT, NE]), ALU.is_ge)
                link(v.tensor_tensor(owns[1], gs, firstf[:, 1:NE + 1].unsqueeze(1).to_broadcast([P, GT, NE]), ALU.is_ge))
                link(v.tensor_tensor(owns[0], owns[0], owns[1], ALU.subtract))
                link(v.scalar_tensor_tensor(out=owns[1], in0=gs, scalar=rows,
                                            in1=base[:, 0:NE].unsqueeze(1).to_broadcast([P, GT, NE]),
                                            op0=ALU.mult, op1=ALU.add))
                link(v.tensor_tensor(owns[0], owns[0], owns[1], ALU.mult))
                link(v.tensor_reduce(rowf, owns[0], AX.X, ALU.add))
                link(v.tensor_copy(chunk_row[:, :], rowf))
                dve.sem_inc(route_ready, 1)

            def experts(l):
                def chunk(g, rows):
                    for half in range(2):
                        cols = slice(256 * half, 256 * half + 256)
                        if rows == P:
                            dve.wait_ge(silu_done[l], 2 * g + 1 + half)
                            ins = v.tensor_tensor(he[:, cols], bank[1 + half][:, 256:512], act_g[:, cols], ALU.mult)
                        else:
                            dve.wait_ge(gu_mm[l], 2 * g + 1 + half)
                            ins = v.tensor_copy(he[:, cols], bank[1 + half][:, 0:256])
                        ins.then_inc(he_ready[l], 1)
                    for half in range(2):
                        kk = slice(2 * half, 2 * half + 2)
                        if rows == P:
                            dve.wait_ge(he_turned[l], 2 * g + 1 + half)
                            ins = v.tensor_copy(he_t[:, kk, :], turned_he(half))
                        else:
                            dve.wait_ge(silu_done[l], 2 * g + 1 + half)
                            ins = v.tensor_tensor(he_t[:, kk, 0:rows], gate_t(half), turned_he(half)[:, :, rows:P],
                                                  ALU.mult)
                        ins.then_inc(het_ready[l], 1)

                chunks(dve, l, chunk)

            def weights(l):
                nt = TOK_TILES[l]
                n16 = NE * nt
                eq, oh1, oh2, sc = (work[:, c:c + n16] for c in (64, 192, 256, 512))
                w1, w2, both = (work[:, 720 + 4 * i:720 + 4 * i + nt] for i in (1, 2, 3))
                for oh, w in ((oh1, w1), (oh2, w2)):
                    link(v.tensor_tensor(eq, oh, sc, ALU.mult))
                    link(v.tensor_reduce(w, eq.rearrange("p (t e) -> p t e", t=nt), AX.X, ALU.add))
                link(v.tensor_tensor(both, w1, w2, ALU.add))
                link(v.reciprocal(both, both))
                v.tensor_tensor(wgt[:, 0:nt], w1, both, ALU.mult)
                v.tensor_tensor(wgt[:, nt:2 * nt], w2, both, ALU.mult)

            def combine(l):
                nt = TOK_TILES[l]
                tb = sum(TOK_TILES[:l])

                def add_rows(tt):
                    dve.wait_ge(c_turned, tb + tt + 1)
                    for k in range(KD):
                        mod = l * NMOD + 5 * KD + k
                        ps = bank[1 + 2 * (tt % 2) + k // 4][:, P * (k % 4):P * (k % 4) + P]
                        xs = x_t[:, k, P * tt:P * tt + P]
                        last = v.scalar_tensor_tensor(out=xs, in0=ps, scalar=mods[:, mod, tt // 2:tt // 2 + 1],
                                                      in1=xs, op0=ALU.mult, op1=ALU.add)
                    last.then_inc(xc_ready, 1)

                for tt in range(nt):
                    dve.wait_ge(y_scaled, tb + tt + 1)
                    v.scalar_tensor_tensor(out=ych[0][:, tt, :], in0=ych[1][:, tt, :],
                                           scalar=wgt[:, nt + tt:nt + tt + 1], in1=ych[0][:, tt, :],
                                           op0=ALU.mult, op1=ALU.add).then_inc(y_summed, 1)
                    if tt >= 1:
                        add_rows(tt - 1)
                add_rows(nt - 1)

            v.memset(yrow, 0.0).then_inc(rows_ready[0], 1)
            dve.sem_inc(rows_ready[1], 1)
            v.memset(eps[:, 0:1], D * EPS)
            v.memset(eps[:, 1:2], HD * EPS)
            v.memset(ones[:, :], 1.0).then_inc(ones_set, 1)
            v.memset(bank[7][:, :], 0.0).then_inc(bank7_set, 1)
            dve.wait_ge(vec_turned, 1)
            v.tensor_copy(vec[:, :], bank[0][:, 0:V_END]).then_inc(vec_ready, 1)
            dve.wait_ge(vec_in, 16 * 15)
            v.memset(ones_b[:, :], 1.0)
            link(v.tensor_copy(upper_b[:, :], upper_f))
            link(v.tensor_scalar(nsink[:, :], sink[:, :], -1.0, None, ALU.mult))
            for k in range(1, KD, 2):
                dve.wait_ge(x_turned, k + 1)
                v.tensor_copy(x_t[:, k, :], bank[1 + k % 6][:, :]).then_inc(xt_dve, 1)
            for u in range(4):
                ada_sum(u)
            add_bias(0, 2 * KD)
            link(v.tensor_scalar(gain[:, 0, 0], mods[:, KD:2 * KD, :], 1.0, D ** 0.5, ALU.add, ALU.mult))
            link(v.tensor_tensor(gain[:, 0, 0], gain[:, 0, 0],
                                 vec[:, V_AG:V_AG + KD].unsqueeze(2).to_broadcast([P, KD, 2]), ALU.mult))
            dve.sem_inc(mods_ready, 1)
            for l in range(DEPTH):
                norm_scale(2 * l, 512)
                qk_norms(l)
                attention(l)
                if l == 0:
                    add_bias(2 * KD, DEPTH * NMOD)
                    gains(0)
                    gains(1)
                    dve.sem_inc(mods_ready, 1)
                add_attention(l)
                norm_scale(2 * l + 1, P * TOK_TILES[l])
                route(l)
                experts(l)
                combine(l)
            for tt in range(2):
                dve.wait_ge(o_turned, tt + 1)
                v.tensor_copy(out_tok[:, tt, 512:D], bank[(6, 7)[tt]][:, :]).then_inc(o_dve, 1)


_INS = ['x', 'c', 'ctx', 'c_ctx', 'ada_w', 'ada_b', 'attn_norm_g', 'ffn_norm_g', 'w_in', 'qn_global', 'kn_global',
        'qn_local', 'kn_local', 'sink_logit', 'w_out', 'router_w', 'router_b', 'w_gate', 'w_up', 'w_down']


def kernel(**inputs):
    import numpy as _np
    import concourse.bacc as _bacc
    from concourse import mybir as _mybir
    from concourse.bass_utils import run_bass_kernel_spmd as _run

    nc = _bacc.Bacc("TRN2", target_bir_lowering=False, num_devices=1)
    arrays, args = {}, []
    for name in _INS:
        a = _np.ascontiguousarray(inputs[name])
        arrays[f"in_{name}_dram"] = a
        args.append(nc.dram_tensor(f"in_{name}_dram", a.shape, _mybir.dt.from_np(a.dtype), kind="ExternalInput").ap())
    a = constants()
    arrays["in_table_dram"] = a
    args.append(nc.dram_tensor("in_table_dram", a.shape, _mybir.dt.from_np(a.dtype), kind="ExternalInput").ap())
    out = nc.dram_tensor("out_dram", (1, SEQ, D), F32, kind="ExternalOutput").ap()
    backbone(nc, *args, out)
    r = _run(nc, [arrays], core_ids=[0])
    return r.results[0]["out_dram"]
```
